# Optimizing a Trainium2 kernel written in Bass

```python
import math
import jax, jax.numpy as jnp
from jax import lax
import numpy as np

D_MODEL = 1024
BATCH = 1
SEQ = 256
DEPTH = 2

N_META = 16
A_HEADS = 8
A_HEAD_DIM = 64
KV_LATENT = 128
IDX_HEADS = 8
IDX_DIM = 64
TOPK_MAX = 256
Q_BLOCK = 128
R_HEADS = 4
R_QK_DIM = 64
R_V_DIM = 128
R_CHUNK = 128
ROPE_BASE = 10000.0
N_EXPERTS = 64
N_GROUPS = 8
TOP_GROUPS = 4
TOP_K = 8
D_EXPERT = 256
D_SHARED = 256
ROUTE_SCALE = 2.5
MOE_BLOCK = 128
DN_ALPHA = (2 * DEPTH) ** 0.25
DN_BETA = (8 * DEPTH) ** -0.25
EPS = 1e-6

IN_COLS = (A_HEADS * A_HEAD_DIM, KV_LATENT, IDX_HEADS * IDX_DIM, IDX_DIM, IDX_HEADS,
           R_HEADS * R_QK_DIM, R_HEADS * R_QK_DIM, R_HEADS * R_V_DIM, R_HEADS * R_V_DIM)
D_IN = sum(IN_COLS)
SPLIT_POINTS = tuple(int(v) for v in np.cumsum(IN_COLS)[:-1])
V_COL_START = SPLIT_POINTS[6]
V_COL_END = SPLIT_POINTS[7]
MIX_WIDTH = A_HEADS * A_HEAD_DIM + R_HEADS * R_V_DIM

kernel_name = "hymba_dsa_retnet_deepnorm_moe"

def layer_norm(x, g, b):
    xf = x.astype(jnp.float32)
    mu = xf.mean(-1, keepdims=True)
    var = jnp.square(xf - mu).mean(-1, keepdims=True)
    return ((xf - mu) * lax.rsqrt(var + EPS) * g + b).astype(x.dtype)

def rms_norm(x, g):
    xf = x.astype(jnp.float32)
    return (xf * lax.rsqrt(jnp.square(xf).mean(-1, keepdims=True) + EPS) * g).astype(x.dtype)

def rotary(x, pos):
    half = x.shape[-1] // 2
    inv = ROPE_BASE ** (-jnp.arange(half, dtype=jnp.float32) / half)
    ang = pos.astype(jnp.float32)[:, None] * inv
    cos = jnp.cos(ang)[None, :, None, :]
    sin = jnp.sin(ang)[None, :, None, :]
    xf = x.astype(jnp.float32)
    x1, x2 = xf[..., :half], xf[..., half:]
    return jnp.concatenate([x1 * cos - x2 * sin, x1 * sin + x2 * cos], -1).astype(x.dtype)

def indexed_sparse_attention(q_lat, c_kv, q_idx, k_idx, w_idx, n_sel):
    b, t = c_kv.shape[:2]
    n_blk = -(-t // Q_BLOCK)
    pad = n_blk * Q_BLOCK - t

    def blocks(a):
        a = jnp.pad(a, [(0, 0), (0, pad)] + [(0, 0)] * (a.ndim - 2))
        return jnp.moveaxis(a.reshape(b, n_blk, Q_BLOCK, *a.shape[2:]), 1, 0)

    key_pos = jnp.arange(t)
    scale = A_HEAD_DIM ** -0.5

    def one_block(args):
        ql, qi, wi, t0 = args
        q_pos = t0 + jnp.arange(Q_BLOCK)
        causal = key_pos[None, :] <= q_pos[:, None]
        rel = jax.nn.relu(jnp.einsum('bqhd,bsd->bqhs', qi, k_idx).astype(jnp.float32))
        score = jnp.einsum('bqh,bqhs->bqs', wi.astype(jnp.float32), rel)
        score = jnp.where(causal[None], score, -jnp.inf)
        _, sel = lax.top_k(score, n_sel)
        valid = sel <= q_pos[None, :, None]
        c_sel = jax.vmap(lambda c, i: c[i])(c_kv, sel)
        logits = jnp.einsum('bqhc,bqkc->bqhk', ql, c_sel).astype(jnp.float32) * scale
        logits = jnp.where(valid[:, :, None, :], logits, -jnp.inf)
        p = jax.nn.softmax(logits, axis=-1).astype(c_sel.dtype)
        return jnp.einsum('bqhk,bqkc->bqhc', p, c_sel)

    t0s = jnp.arange(n_blk) * Q_BLOCK
    o = lax.map(one_block, (blocks(q_lat), blocks(q_idx), blocks(w_idx), t0s))
    o = jnp.moveaxis(o, 0, 1).reshape(b, n_blk * Q_BLOCK, *o.shape[3:])
    return o[:, :t]

def chunkwise_retention(q, k, v):
    b, t, h, dk = q.shape
    dv = v.shape[-1]
    n_c = -(-t // R_CHUNK)
    pad = n_c * R_CHUNK - t

    def chunks(a):
        a = jnp.pad(a.astype(jnp.float32), [(0, 0), (pad, 0), (0, 0), (0, 0)])
        return a.reshape(b, n_c, R_CHUNK, h, a.shape[-1]).transpose(1, 0, 3, 2, 4)

    log_g = jnp.log1p(-jnp.exp(jnp.linspace(math.log(1.0 / 32), math.log(1.0 / 512), R_HEADS))).astype(jnp.float32)
    idx = jnp.arange(R_CHUNK, dtype=jnp.float32)
    diff = idx[:, None] - idx[None, :]
    decay_mat = jnp.where(diff[None] >= 0, jnp.exp(diff[None] * log_g[:, None, None]), 0.0)
    q_decay = jnp.exp((idx + 1.0)[None, :] * log_g[:, None])[:, :, None]
    k_decay = jnp.exp((R_CHUNK - 1.0 - idx)[None, :] * log_g[:, None])[:, :, None]
    chunk_decay = jnp.exp(R_CHUNK * log_g)[:, None, None]

    def step(state, qkv):
        qc, kc, vc = qkv
        inner = jnp.einsum('bhnd,bhmd->bhnm', qc, kc) * decay_mat
        out = (jnp.einsum('bhnm,bhmv->bhnv', inner, vc)
               + jnp.einsum('bhnd,bhdv->bhnv', qc, state) * q_decay)
        state = chunk_decay * state + jnp.einsum('bhmd,bhmv->bhdv', kc * k_decay, vc)
        return state, out

    state0 = jnp.zeros((b, h, dk, dv), jnp.float32)
    _, o = lax.scan(step, state0, (chunks(q), chunks(k), chunks(v)))
    o = o.transpose(1, 0, 3, 2, 4).reshape(b, n_c * R_CHUNK, h, dv)
    return o[:, pad:]

def hybrid_mixer(x, w_in, w_uk, w_uv, kv_norm_w, ret_norm_w, w_o, n_sel):
    b, t, _ = x.shape
    proj = x @ w_in
    qa, ckv, qi, ki, wi, qr, kr, vr, gr = jnp.split(proj, SPLIT_POINTS, axis=-1)
    qa = qa.reshape(b, t, A_HEADS, A_HEAD_DIM)
    ckv = rms_norm(ckv, kv_norm_w)
    q_lat = jnp.einsum('bthd,hdc->bthc', qa, w_uk)
    o_lat = indexed_sparse_attention(q_lat, ckv, qi.reshape(b, t, IDX_HEADS, IDX_DIM), ki,
                                     wi * (IDX_HEADS ** -0.5), n_sel)
    out_a = jnp.einsum('bthc,hcd->bthd', o_lat, w_uv).reshape(b, t, A_HEADS * A_HEAD_DIM)
    pos = jnp.arange(t)
    qr = rotary(qr.reshape(b, t, R_HEADS, R_QK_DIM), pos)
    kr = rotary(kr.reshape(b, t, R_HEADS, R_QK_DIM), pos) * (R_QK_DIM ** -0.5)
    o_r = chunkwise_retention(qr, kr, vr.reshape(b, t, R_HEADS, R_V_DIM))
    mu = o_r.mean(-1, keepdims=True)
    var = jnp.square(o_r - mu).mean(-1, keepdims=True)
    o_r = ((o_r - mu) * lax.rsqrt(var + EPS)).reshape(b, t, R_HEADS * R_V_DIM) * ret_norm_w
    out_b = jax.nn.silu(gr) * o_r.astype(x.dtype)
    return jnp.concatenate([out_a, out_b], axis=-1) @ w_o

def routed_experts(xf, top_idx, top_w, w_gate, w_up, w_down):
    n_tok, d = xf.shape
    n_assign = n_tok * TOP_K
    n_blocks = -(-n_assign // MOE_BLOCK) + N_EXPERTS
    n_rows = n_blocks * MOE_BLOCK
    expert_flat = top_idx.reshape(-1)
    token_flat = jnp.arange(n_assign, dtype=jnp.int32) // TOP_K
    gate_flat = top_w.reshape(-1)
    order = jnp.argsort(expert_flat)
    e_sorted = expert_flat[order]
    counts = jnp.bincount(expert_flat, length=N_EXPERTS)
    blocks_per_e = (counts + MOE_BLOCK - 1) // MOE_BLOCK
    blk_end = jnp.cumsum(blocks_per_e)
    blk_start = blk_end - blocks_per_e
    seg_start = jnp.cumsum(counts) - counts
    row = blk_start[e_sorted] * MOE_BLOCK + (jnp.arange(n_assign) - seg_start[e_sorted])
    row_token = jnp.zeros((n_rows,), jnp.int32).at[row].set(token_flat[order])
    row_gate = jnp.zeros((n_rows,), xf.dtype).at[row].set(gate_flat[order].astype(xf.dtype))
    block_expert = jnp.minimum(jnp.searchsorted(blk_end, jnp.arange(n_blocks), side='right'),
                               N_EXPERTS - 1)
    x_rows = xf[row_token].reshape(n_blocks, MOE_BLOCK, d)

    def block_ffn(args):
        xb, e = args
        hdn = jax.nn.silu(xb @ w_gate[e]) * (xb @ w_up[e])
        return hdn @ w_down[e]

    y_rows = lax.map(block_ffn, (x_rows, block_expert)).reshape(n_rows, d)
    return jax.ops.segment_sum(y_rows * row_gate[:, None], row_token, num_segments=n_tok)

def moe_ffn(x, w_router, router_bias, w_gate, w_up, w_down, ws_gate, ws_up, ws_down):
    b, t, d = x.shape
    xf = x.reshape(-1, d)
    scores = jax.nn.sigmoid((xf @ w_router).astype(jnp.float32))
    sel_scores = scores + router_bias.astype(jnp.float32)
    grp = sel_scores.reshape(-1, N_GROUPS, N_EXPERTS // N_GROUPS)
    grp_score = lax.top_k(grp, 2)[0].sum(-1)
    _, top_grp = lax.top_k(grp_score, TOP_GROUPS)
    grp_mask = jnp.any(top_grp[..., None] == jnp.arange(N_GROUPS), axis=-2)
    expert_mask = jnp.repeat(grp_mask, N_EXPERTS // N_GROUPS, axis=-1)
    _, top_idx = lax.top_k(jnp.where(expert_mask, sel_scores, -jnp.inf), TOP_K)
    gates = jnp.take_along_axis(scores, top_idx, axis=-1)
    gates = gates / gates.sum(-1, keepdims=True) * ROUTE_SCALE
    routed = routed_experts(xf, top_idx, gates, w_gate, w_up, w_down)
    shared = (jax.nn.silu(xf @ ws_gate) * (xf @ ws_up)) @ ws_down
    return (routed + shared).reshape(b, t, d)

def setup_inputs(seed: int = 0) -> dict:
    key = jax.random.key(seed)
    ks = jax.random.split(key, 24)
    L = DEPTH

    def nrm(k, shape, scale):
        return jax.random.normal(k, shape, jnp.float32) * scale

    x = nrm(ks[0], (BATCH, SEQ, D_MODEL), 1.0)
    meta_tokens = nrm(ks[1], (N_META, D_MODEL), 1.0)
    w_in = nrm(ks[2], (L, D_MODEL, D_IN), D_MODEL ** -0.5)
    w_in = w_in.at[:, :, V_COL_START:V_COL_END].multiply(DN_BETA)
    w_uk = nrm(ks[3], (L, A_HEADS, A_HEAD_DIM, KV_LATENT), KV_LATENT ** -0.5)
    w_uv = nrm(ks[4], (L, A_HEADS, KV_LATENT, A_HEAD_DIM), KV_LATENT ** -0.5 * DN_BETA)
    kv_norm_w = 1.0 + nrm(ks[5], (L, KV_LATENT), 0.02)
    ret_norm_w = 1.0 + nrm(ks[6], (L, R_HEADS * R_V_DIM), 0.02)
    w_o = nrm(ks[7], (L, MIX_WIDTH, D_MODEL), MIX_WIDTH ** -0.5 * DN_BETA)
    ln1_g = 1.0 + nrm(ks[8], (L, D_MODEL), 0.02)
    ln1_b = nrm(ks[9], (L, D_MODEL), 0.02)
    w_router = nrm(ks[10], (L, D_MODEL, N_EXPERTS), D_MODEL ** -0.5)
    router_bias = nrm(ks[11], (L, N_EXPERTS), 0.01)
    w_gate = nrm(ks[12], (L, N_EXPERTS, D_MODEL, D_EXPERT), D_MODEL ** -0.5)
    w_up = nrm(ks[13], (L, N_EXPERTS, D_MODEL, D_EXPERT), D_MODEL ** -0.5)
    w_down = nrm(ks[14], (L, N_EXPERTS, D_EXPERT, D_MODEL), D_EXPERT ** -0.5 * DN_BETA)
    ws_gate = nrm(ks[15], (L, D_MODEL, D_SHARED), D_MODEL ** -0.5)
    ws_up = nrm(ks[16], (L, D_MODEL, D_SHARED), D_MODEL ** -0.5)
    ws_down = nrm(ks[17], (L, D_SHARED, D_MODEL), D_SHARED ** -0.5 * DN_BETA)
    ln2_g = 1.0 + nrm(ks[18], (L, D_MODEL), 0.02)
    ln2_b = nrm(ks[19], (L, D_MODEL), 0.02)
    return {"x": x, "meta_tokens": meta_tokens, "w_in": w_in, "w_uk": w_uk, "w_uv": w_uv,
            "kv_norm_w": kv_norm_w, "ret_norm_w": ret_norm_w, "w_o": w_o,
            "ln1_g": ln1_g, "ln1_b": ln1_b, "w_router": w_router, "router_bias": router_bias,
            "w_gate": w_gate, "w_up": w_up, "w_down": w_down,
            "ws_gate": ws_gate, "ws_up": ws_up, "ws_down": ws_down,
            "ln2_g": ln2_g, "ln2_b": ln2_b}

def reference(x, meta_tokens, w_in, w_uk, w_uv, kv_norm_w, ret_norm_w, w_o, ln1_g, ln1_b,
              w_router, router_bias, w_gate, w_up, w_down, ws_gate, ws_up, ws_down,
              ln2_g, ln2_b):
    b, s, d = x.shape
    n_sel = min(TOPK_MAX, s // 4)
    meta = jnp.broadcast_to(meta_tokens.astype(x.dtype)[None], (b, N_META, d))
    h = jnp.concatenate([meta, x], axis=1)
    for l in range(DEPTH):
        mix = hybrid_mixer(h, w_in[l], w_uk[l], w_uv[l], kv_norm_w[l], ret_norm_w[l], w_o[l], n_sel)
        h = layer_norm(DN_ALPHA * h + mix, ln1_g[l], ln1_b[l])
        ffn = moe_ffn(h, w_router[l], router_bias[l], w_gate[l], w_up[l], w_down[l],
                      ws_gate[l], ws_up[l], ws_down[l])
        h = layer_norm(DN_ALPHA * h + ffn, ln2_g[l], ln2_b[l])
    return h[:, N_META:]


_drawn_inputs = setup_inputs


def setup_inputs(seed=0):
    import zlib

    import numpy as np

    out = dict(_drawn_inputs(seed))
    spreads = {}
    factors = {'kv_norm_w': 8.0, 'ret_norm_w': 3.068}
    for name, (base, spread) in spreads.items():
        noise = np.random.default_rng([zlib.crc32(name.encode()), seed]).standard_normal(out[name].shape)
        drawn = base * np.exp(spread * noise) if base else spread * noise
        out[name] = __import__('jax').numpy.asarray(drawn.astype(out[name].dtype))
    for name, factor in factors.items():
        out[name] = (out[name] * factor).astype(out[name].dtype)
    return out
```

```python
from contextlib import ExitStack

import numpy as np

import concourse.bass as bass
from concourse import mybir

F32 = mybir.dt.float32
I32 = mybir.dt.int32
ALU = mybir.AluOpType
ACT = mybir.ActivationFunctionType
AX = mybir.AxisListType.X

D = 1024
SEQ = 256
DEPTH = 2
META = 16
T = META + SEQ
A_HEADS, A_DIM, LAT = 8, 64, 128
I_HEADS = 8
N_SEL = min(256, SEQ // 4)
R_HEADS, R_QK, R_V = 4, 64, 128
E, GROUPS, TOP_GROUPS = 64, 8, 4
F = 256
EPS = 1e-6
ALPHA = (2 * DEPTH) ** 0.25
ROUTE_SCALE = 2.5
D_IN = 2760
KC = D // 128

CHUNKS = [(0, 16), (16, 128), (144, 128)]
KEYS = [16, 144, 272]
CAP = 64
EXTRA = 4
ROUNDS = 1 + EXTRA
PAIRS = E // 2
E_PAD = E + 4
FAR = 4096.0
NEG = -1e30
TAKEN = -3e38

BLOCKS = [(128 * b, 128) for b in range(9)] + [(1152, 72)] + [(1224 + 128 * b, 128) for b in range(12)]
DOUBLES = [(0, 512, range(0, 4)), (512, 1024, range(4, 8)), (1024, 1480, range(8, 12)),
           (1480, 1992, range(12, 16)), (1992, 2504, range(16, 20)), (2504, 2760, range(20, 22))]
DOUBLE_SLOT = [3, 4, 5, 0, 1, 2]
STAGES = 6
SLOT_LOADS = [n + PAIRS // 2 * ROUNDS for n in (1, 1, 2, 2, 2, 3)]

CONSTS = [("ident", 128), ("before", 128), ("ones", 128), ("cos", 96), ("sin", 96), ("decay", 4 * T),
          ("causal", 144 + 272), ("causal0", 16), ("iota", CAP), ("code", 3), ("iota_t", T), ("tri", 64)]
N_CONST = sum(n for _, n in CONSTS)


def shape_constants():
    p = np.arange(128)
    c = {"ident": np.eye(128), "before": p[:, None] < p[None, :], "ones": np.ones((128, 128))}
    half = R_QK // 2
    inv = (np.float32(10000.0) ** (-np.arange(half, dtype=np.float32) / np.float32(half))).astype(np.float32)
    cos, sin = np.zeros((128, 3, half)), np.zeros((128, 3, half))
    for n, (t0, w) in enumerate(CHUNKS):
        ang = ((t0 + p).astype(np.float32)[:, None] * inv).astype(np.float32).astype(np.float64)
        cos[:, n], sin[:, n] = np.cos(ang), np.sin(ang)
    c["cos"], c["sin"] = cos.reshape(128, -1), sin.reshape(128, -1)
    log_g = np.log1p(-np.exp(np.linspace(np.log(1.0 / 32), np.log(1.0 / 512), R_HEADS)))
    ahead = np.arange(T)[None, :] - p[:, None]
    c["decay"] = np.concatenate([np.where(ahead >= 0, np.exp(np.maximum(ahead, 0) * g) * R_QK ** -0.5, 0.0)
                                 for g in log_g], axis=1)
    c["causal"] = np.concatenate([np.where(np.arange(KEYS[n])[None, :] <= CHUNKS[n][0] + p[:, None], 0.0, NEG)
                                  for n in (1, 2)], axis=1)
    c["causal0"] = np.where(np.arange(16)[None, :] <= (p % 16)[:, None], 0.0, NEG)
    c["iota"] = np.tile(np.arange(CAP), (128, 1))
    c["code"] = np.stack([t0 + p - FAR for t0, _ in CHUNKS], axis=1)
    c["iota_t"] = np.tile(np.arange(T) - FAR, (128, 1))
    c["tri"] = np.tile((np.arange(8)[None, :] < np.arange(8)[:, None]).reshape(1, 64), (128, 1))
    return np.concatenate([np.asarray(c[n], np.float64) for n, _ in CONSTS], axis=1).astype(np.float32)


def acc_segments(d):
    out, at, end = [], d * T, (d + 1) * T
    while at < end:
        n = min(end, (at // 512 + 1) * 512) - at
        out.append((at // 512, at % 512, at - d * T, n))
        at += n
    return out


def decoder_kernel(nc, a, out):
    ctx = ExitStack()
    with ctx:
        def sb(name, shape, dt=F32):
            return ctx.enter_context(nc.sbuf_tensor(name, shape, dt))

        def sem(name):
            return ctx.enter_context(nc.semaphore(name))

        bank = [ctx.enter_context(nc.psum_tensor(f"bank{i}", [128, 512], F32)) for i in range(8)]

        ring = sb("ring", [128, 6, 4096])
        const = sb("const", [128, N_CONST])
        h_tok = sb("h_tok", [128, 3, D])
        hT = sb("hT", [128, KC, T])
        ln_par = sb("ln_par", [128, 2, D])
        wuk = sb("wuk", [128, 4, LAT])
        wuv = sb("wuv", [128, 8, 64])
        wr = sb("wr", [128, KC * E])
        kvn_w = sb("kvn_w", [128, LAT])
        retn_w = sb("retn_w", [128, R_HEADS * R_V])
        rbias = sb("rbias", [128, E])
        half_pow = sb("half_pow", [128, 12])
        ssq = sb("ssq", [128, 3])
        ckv_var = sb("ckv_var", [128, 3])
        ckv_rstd = sb("ckv_rstd", [128, 3])
        ret_stats = sb("ret_stats", [128, 12, 6])
        ret_mv = sb("ret_mv", [128, 12, 2])
        ret_var = sb("ret_var", [128, 12])
        ret_rstd = sb("ret_rstd", [128, 12])
        ln_stats = sb("ln_stats", [128, 3, 12])
        ln_mv = sb("ln_mv", [128, 3, 2])
        ln_var = sb("ln_var", [128, 3])
        ln_rstd = sb("ln_rstd", [128, 3])
        ln_shift = sb("ln_shift", [128, 3])
        row_max = sb("row_max", [128, 17])
        neg_max = sb("neg_max", [128, 17])
        row_sum = sb("row_sum", [128, 17])
        row_inv = sb("row_inv", [128, 17])
        best8 = sb("best8", [128, 8])

        REGION = 15232
        region = sb("region", [128, REGION])

        def carve(sizes):
            at, views = 0, {}
            for name, n in sizes:
                views[name] = region[:, at:at + n]
                at += n
            assert at <= REGION, at
            return views

        mx = carve([("qa", 4 * T), ("qi", 4 * T), ("kw", T), ("kd", T), ("stage", STAGES * T), ("ckv", 3 * 128),
                    ("ckvT", T), ("wi", 24), ("rot", 3 * 512), ("tmp", 4 * T), ("v", 3 * 512), ("gate", 3 * 512),
                    ("rl", 2 * T), ("qk", 4 * T), ("lat", 8 * T), ("mask", 416), ("work", T)])
        qaT = mx["qa"].rearrange("p (b t) -> p b t", t=T)
        qiT = mx["qi"].rearrange("p (b t) -> p b t", t=T)
        kwT, kdT = mx["kw"], mx["kd"]
        stage = mx["stage"].rearrange("p (b t) -> p b t", t=T)
        ckv = mx["ckv"].rearrange("p (c f) -> p c f", c=3)
        ckvT = mx["ckvT"]
        wi = mx["wi"].rearrange("p (c h) -> p c h", c=3)
        rot = mx["rot"].rearrange("p (c f) -> p c f", c=3)
        rot_a, rot_b = mx["tmp"][:, 0:512], mx["tmp"][:, 512:1024]
        v_tok = mx["v"].rearrange("p (c f) -> p c f", c=3)
        gate = mx["gate"].rearrange("p (c f) -> p c f", c=3)
        rl = mx["rl"].rearrange("p (b t) -> p b t", t=T)
        sg_tmp = mx["rl"][:, 0:512]
        qkT = mx["qk"].rearrange("p (b t) -> p b t", t=T)
        latT = mx["lat"].rearrange("p (h t) -> p h t", t=T)
        masks = {1: mx["mask"][:, 0:144], 2: mx["mask"][:, 144:416]}
        work = mx["work"]
        mixT = [qaT[:, b, :] for b in range(4)] + [qkT[:, b, :] for b in range(4)]
        decayed = mx["stage"][:, 0:1312].rearrange("p (b n) -> p b n", b=2)
        logit = mx["tmp"].rearrange("p (b t) -> p b t", t=T)
        pT = region[:, 4 * T:4 * T + 4 * 384].rearrange("p (b j q) -> p b j q", b=4, j=3)
        o_ret = rot

        mo = carve([("xg", 2 * D), ("xgT", 2 * 1024), ("y", 2 * 1024), ("selg", 2 * T), ("sel", 384), ("pb", 18), ("idg", 4),
                    ("route", 3 * E_PAD * 3), ("score", 192), ("biased", 192), ("best2", 192), ("grp", 24),
                    ("gt", 192), ("eq", 192), ("rank", 24), ("picked", 192), ("chosen", 192), ("tmp", 192),
                    ("gsum", 3), ("ginv", 3), ("cmax", 1), ("sg", 256), ("ha", 256), ("h", 256), ("h2", 256),
                    ("sgs", 2 * T), ("hs", 2 * T), ("hsT", 2 * T), ("accT", 8 * T)])
        xg = mo["xg"].rearrange("p (b n) -> p b n", b=2)
        xgT = mo["xgT"].rearrange("p (b k s) -> p b k s", b=2, k=KC)
        y_sb = mo["y"].rearrange("p (b n) -> p b n", b=2)
        selg = mo["selg"].rearrange("p (b t) -> p b t", b=2)
        sel = mo["sel"].rearrange("p (c e s) -> p c e s", c=3, e=2)
        pb = mo["pb"].rearrange("p (c e v) -> p c e v", c=3, e=2)
        idg = mo["idg"].rearrange("p (b v) -> p b v", b=2)
        route = mo["route"].rearrange("p (c e v) -> p c e v", c=3, v=3)
        route_pairs = mo["route"].rearrange("p (c n) -> p c n", c=3)
        rows3 = {n: mo[n].rearrange("p (c e) -> p c e", c=3)
                 for n in ("score", "biased", "best2", "grp", "rank", "picked", "chosen", "tmp")}
        cube = {n: mo[n].rearrange("p (c g e) -> p c g e", c=3, g=8) for n in ("best2", "gt", "eq", "biased")}
        sgs = mo["sgs"].rearrange("p (j t) -> p j t", j=2)
        hs = mo["hs"].rearrange("p (j t) -> p j t", j=2)
        hsT = mo["hsT"].rearrange("p (j t) -> p j t", j=2)
        accT = mo["accT"]
        rank_i = sb("rank_i", [128, 2], I32)
        count_i = sb("count_i", [1, 1], I32)

        k, at = {}, 0
        for name, n in CONSTS:
            k[name] = const[:, at:at + n]
            at += n
        decay = k["decay"].rearrange("p (h t) -> p h t", h=4)
        causal = {1: k["causal"][:, 0:144], 2: k["causal"][:, 144:416]}
        cos3 = k["cos"].rearrange("p (c f) -> p c f", c=3)
        sin3 = k["sin"].rearrange("p (c f) -> p c f", c=3)

        h_rows = nc.dram_tensor("h_rows", [T, D], F32, kind="Internal").ap()

        const_in = sem("const_in")
        h_in = sem("h_in")
        slot_in = [sem(f"slot_in{s}") for s in range(6)]
        small_mix = sem("small_mix")
        small_moe = sem("small_moe")
        ln_par_in = sem("ln_par_in")
        proj_done = sem("proj_done")
        proj_act = sem("proj_act")
        proj_dve = sem("proj_dve")
        lat_done = sem("lat_done")
        lat_act = sem("lat_act")
        lat_dve = sem("lat_dve")
        ckv_turned = sem("ckv_turned")
        ckv_ssq = sem("ckv_ssq")
        ckv_var_ready = sem("ckv_var_ready")
        ckv_rstd_ready = sem("ckv_rstd_ready")
        ckv_ready = sem("ckv_ready")
        ckvT_done = sem("ckvT_done")
        ckvT_ready = sem("ckvT_ready")
        wi_turned = sem("wi_turned")
        wi_ready = sem("wi_ready")
        q0_ready = sem("q0_ready")
        index_done = sem("index_done")
        index_relu = sem("index_relu")
        index_added = sem("index_added")
        tok_turned = sem("tok_turned")
        tok_copied = sem("tok_copied")
        gate_sig = sem("gate_sig")
        rot_ready = sem("rot_ready")
        gate_mul = sem("gate_mul")
        gate_ready = sem("gate_ready")
        ret_scores = sem("ret_scores")
        ret_decayed = sem("ret_decayed")
        ret_out = sem("ret_out")
        ret_var_ready = sem("ret_var_ready")
        ret_rstd_ready = sem("ret_rstd_ready")
        ret_ready = sem("ret_ready")
        ret_turned = sem("ret_turned")
        ret_mix = sem("ret_mix")
        logits_done = sem("logits_done")
        logits_masked = sem("logits_masked")
        max_ready = sem("max_ready")
        exp_done = sem("exp_done")
        inv_ready = sem("inv_ready")
        prob_ready = sem("prob_ready")
        prob_turned = sem("prob_turned")
        prob_copied = sem("prob_copied")
        olat_done = sem("olat_done")
        olat_ready = sem("olat_ready")
        out_a_done = sem("out_a_done")
        out_a_ready = sem("out_a_ready")
        sub_done = sem("sub_done")
        z_ready = sem("z_ready")
        ln_var_ready = sem("ln_var_ready")
        ln_rstd_ready = sem("ln_rstd_ready")
        ln_shift_ready = sem("ln_shift_ready")
        ln_norm = sem("ln_norm")
        ln_scaled = sem("ln_scaled")
        ln_ready = sem("ln_ready")
        hT_turned = sem("hT_turned")
        hT_act = sem("hT_act")
        hT_dve = sem("hT_dve")
        h_stored = sem("h_stored")
        moe_clear = sem("moe_clear")
        moe_coded = sem("moe_coded")
        router_done = sem("router_done")
        score_ready = sem("score_ready")
        chosen_ready = sem("chosen_ready")
        gates_ready = sem("gates_ready")
        rank_done = sem("rank_done")
        rank_ready = sem("rank_ready")
        count_ready = sem("count_ready")
        shared_done = sem("shared_done")
        shared_sig = sem("shared_sig")
        shared_ready = sem("shared_ready")
        shared_down = sem("shared_down")
        gates_used = sem("gates_used")
        gu_done = sem("gu_done")
        xta_done = sem("xta_done")
        xtb_done = sem("xtb_done")
        ht_done = sem("ht_done")
        y_done = sem("y_done")
        scattered = sem("scattered")
        slot_row_done = sem("slot_row_done")
        sig_ready = sem("sig_ready")
        xta_ready = sem("xta_ready")
        y_ready = sem("y_ready")
        shifted = sem("shifted")
        selg_ready = sem("selg_ready")
        pair_ready = sem("pair_ready")
        sel_ready = sem("sel_ready")
        ha_ready = sem("ha_ready")
        h_ready = sem("h_ready")
        xtb_ready = sem("xtb_ready")
        ht_ready = sem("ht_ready")
        idg_ready = sem("idg_ready")
        slot_row_ready = sem("slot_row_ready")
        gathered = [sem(f"gathered{i}") for i in range(2)]
        acc_act = sem("acc_act")
        acc_dve = sem("acc_dve")
        out_stored = sem("out_stored")
        act_step = sem("act_step")
        dve_step = sem("dve_step")
        pool_step = sem("pool_step")
        passed = sem("passed")

        def hold_here(eng, s, value):
            eng.wait_ge(s, value)
            eng.sem_inc(passed, 1)

        w_in_v = a["w_in"].rearrange("l (p k) n -> l p k n", k=KC)
        w_o_v = a["w_o"].rearrange("l (k p) n -> l p k n", p=128)
        gate_v = a["w_gate"].rearrange("l (q e) (p k) f -> (l q) p e (k f)", e=2, k=KC)
        up_v = a["w_up"].rearrange("l (q e) (p k) f -> (l q) p e (k f)", e=2, k=KC)
        down_v = a["w_down"].rearrange("l (q e) (j p) n -> (l q) p (e j) n", e=2, p=128)
        wsg_v = a["ws_gate"].rearrange("l (p k) f -> l p (k f)", k=KC)
        wsu_v = a["ws_up"].rearrange("l (p k) f -> l p (k f)", k=KC)
        wsd_v = a["ws_down"].rearrange("l (j p) n -> l p j n", p=128)

        def of_layer(v, l):
            names = " ".join(f"d{i}" for i in range(len(v.shape) - 1))
            return v[bass.ds(l, 1)].rearrange(f"l {names} -> (l {names.split()[0]}) {' '.join(names.split()[1:])}")

        def slot(s, at, n):
            return ring[:, s, at:at + n]

        block = ctx.enter_context(nc.Block())

        @block.sync
        def _(sp):
            sp.dma_start(const[:], a["consts"]).then_inc(const_in, 16)
            sp.dma_start(h_tok[0:META, 0, :], a["meta_tokens"]).then_inc(h_in, 16)
            sp.dma_start(h_tok[:, 1:3, :], a["x"].rearrange("b (c p) d -> p (b c) d", p=128)).then_inc(h_in, 16)

            def load_pair(l, r, i, u, part, first):
                g = l * ROUNDS + r
                s = part if u == 0 else 3 + part
                if not first:
                    used, per = ((gates_used, 1), (gu_done, 1), (y_done, 2))[part]
                    sp.wait_ge(used, per * (g * PAIRS + i * 2 + u - 1))
                q = l * PAIRS + i * 2 + u
                src = (gate_v, up_v, down_v)[part][bass.ds(q, 1)]
                if part < 2:
                    src = src.rearrange("o p e n -> (o p) e n")
                    dst = ring[:, s, :].rearrange("p (e n) -> p e n", e=2)
                else:
                    src = src.rearrange("o p e n -> (o p) e n")
                    dst = ring[:, s, :].rearrange("p (e n) -> p e n", e=4)
                sp.dma_start(dst, src).then_inc(slot_in[s], 16)

            with sp.Fori(0, DEPTH) as l:
                for n, (c0, c1, _) in enumerate(DOUBLES):
                    if n == 0:
                        sp.wait_ge(y_done, l * (2 * PAIRS * ROUNDS))
                    s, w = DOUBLE_SLOT[n], c1 - c0
                    src = w_in_v[bass.ds(l, 1), :, :, c0:c1].rearrange("l p k n -> (l p) k n")
                    sp.dma_start(slot(s, 0, KC * w).rearrange("p (k n) -> p k n", k=KC), src).then_inc(slot_in[s], 16)
                sp.dma_start(slot(2, 2048, 2048).rearrange("p (j n) -> p j n", j=2),
                             wsd_v[bass.ds(l, 1)].rearrange("l p j n -> (l p) j n")).then_inc(slot_in[2], 16)
                for n in range(2):
                    sp.wait_ge(proj_done, l * 22 + 4 * (n + 1))
                    src = w_o_v[bass.ds(l, 1), :, 4 * n:4 * n + 4, :].rearrange("l p k n -> (l p) k n")
                    sp.dma_start(ring[:, 3 + n, :].rearrange("p (k n) -> p k n", k=4), src).then_inc(slot_in[3 + n], 16)
                sp.wait_ge(proj_done, l * 22 + 12)
                sp.dma_start(slot(5, 0, 2048), wsg_v[bass.ds(l, 1)].rearrange("l p n -> (l p) n")).then_inc(slot_in[5], 16)
                sp.dma_start(slot(5, 2048, 2048), wsu_v[bass.ds(l, 1)].rearrange("l p n -> (l p) n")).then_inc(slot_in[5], 16)
                sp.wait_ge(proj_done, l * 22 + 16)
                load_pair(l, 0, 0, 0, 0, True)
                sp.wait_ge(proj_done, l * 22 + 20)
                load_pair(l, 0, 0, 0, 1, True)
                sp.wait_ge(sub_done, l * 6 + 3)
                load_pair(l, 0, 0, 1, 0, True)
                load_pair(l, 0, 0, 1, 1, True)
                sp.wait_ge(shared_down, l + 1)
                load_pair(l, 0, 0, 0, 2, True)
                load_pair(l, 0, 0, 1, 2, True)
                with sp.Fori(1, PAIRS // 2) as i:
                    for u in range(2):
                        for part in range(3):
                            load_pair(l, 0, i, u, part, False)
                hold_here(sp, count_ready, l + 1)
                most = sp.value_load(count_i[0:1, 0:1], min_val=0, max_val=T)
                with sp.If(most > CAP):
                    with sp.Fori(1, ROUNDS) as r:
                        with sp.Fori(0, PAIRS // 2) as i:
                            for u in range(2):
                                for part in range(3):
                                    load_pair(l, r, i, u, part, False)
                with sp.Else():
                    for s in range(6):
                        sp.wait_ge(slot_in[s], l * (16 * SLOT_LOADS[s]) + 16 * (SLOT_LOADS[s] - 16 * EXTRA))
                        sp.sem_inc(slot_in[s], 16 * 16 * EXTRA)
            sp.wait_ge(ln_ready, DEPTH * 6)
            sp.dma_start(out.rearrange("b (c p) d -> p (b c) d", p=128), h_tok[:, 1:3, :]).then_inc(out_stored, 16)
            sp.wait_ge(out_stored, 16)

        @block.tensor
        def _(pe):
            ident = k["ident"]
            mm = pe.matmul

            def turn_h():
                for n, (t0, w) in enumerate(CHUNKS):
                    rows = h_tok[0:w, n, :].rearrange("t (p k) -> t k p", k=KC)
                    for half in range(1 if n == 0 else 2):
                        per = KC if n == 0 else 4
                        for j in range(per):
                            last = pe.transpose(bank[2 * n + half][:, j * w:(j + 1) * w], rows[:, half * 4 + j, :],
                                                ident[0:w, 0:w])
                        last.then_inc(hT_turned, 1)

            rounds_run = pe.alloc_register("rounds_run")
            pe.reg_mov(rounds_run, 0)

            pe.wait_ge(const_in, 16)
            pe.wait_ge(h_in, 32)
            turn_h()

            def round_(l, r, extra):
                g = l * ROUNDS + r
                past = pe.snap(rounds_run)
                def slot_rows(q, before, evac):
                    pe.wait_ge(before, evac)
                    pe.wait_ge(sel_ready, g * 34 + q + 1)
                    for e in range(2):
                        for n, (t0, w) in enumerate(CHUNKS):
                            last = mm(bank[7][64 * e:64 * e + 64, 0:2], sel[0:w, n, e, :], pb[0:w, n, e, 0:2],
                                      start=(n == 0), stop=(n == 2))
                    last.then_inc(slot_row_done, 1)

                def turn_x(q, u, part, before, evac):
                    pe.wait_ge(before, evac)
                    rows = xg[:, u, :].rearrange("s (p k) -> s k p", k=KC)
                    for j in range(4):
                        last = pe.transpose(bank[7][:, j * 128:(j + 1) * 128], rows[:, 4 * part + j, :], ident)
                    last.then_inc((xta_done, xtb_done)[part], 1)

                def scatter(u, ds, last_of_pair, stop=False):
                    for d in ds:
                        for b, c, t, n in acc_segments(d):
                            last = mm(bank[b][:, c:c + n], y_sb[:, u, d * 128:(d + 1) * 128], selg[:, u, t:t + n],
                                      start=False, stop=stop, skip_group_check=True)
                    if last_of_pair:
                        last.then_inc(scattered, 1)

                slot_rows(0, slot_row_ready, g * 34)
                slot_rows(1, slot_row_ready, g * 34 + 1)
                pe.wait_ge(gathered[0], past * (16 * 17) + 16)
                turn_x(0, 0, 0, slot_row_ready, g * 34 + 2)
                turn_x(0, 0, 1, xta_ready, g * 33 + 1)

                with pe.Fori(0, PAIRS // 2) as i:
                    for u in range(2):
                        p = i * 2 + u
                        base = 0 if u == 0 else 3
                        before = [SLOT_LOADS[base + j] - 16 * ROUNDS for j in range(3)]
                        arrived = [l * (16 * SLOT_LOADS[base + j]) + r * 256 + i * 16
                                   + 16 * (before[j] + 1) for j in range(3)]
                        pe.wait_ge(slot_in[base], arrived[0])
                        pe.wait_ge(xtb_ready, g * 33 + p + 1)
                        pe.wait_ge(xta_ready, g * 33 + p + 1)
                        pe.wait_ge(h_ready, g * 32 + p)
                        for part in range(2):
                            if part == 1:
                                pe.wait_ge(slot_in[base + 1], arrived[1])
                            w = ring[:, base + part, :].rearrange("p (e k f) -> p e k f", e=2, k=KC)
                            for kk in range(KC):
                                for e in range(2):
                                    last = mm(bank[5][64 * e:64 * e + 64, part * F:(part + 1) * F],
                                              xgT[:, u, kk, 64 * e:64 * e + 64], w[:, e, kk, :],
                                              start=(kk == 0), stop=(kk == KC - 1))
                            last.then_inc((gates_used, gu_done)[part], 1)
                        pe.wait_ge(gathered[1 - u], past * (16 * 17) + ((i + u) * 16 + 16))
                        turn_x(p + 1, 1 - u, 0, slot_row_ready, g * 34 + p + 2)
                        pe.wait_ge(y_ready, g * 64 + p * 2)
                        pe.wait_ge(selg_ready, g * 33 + p + 1)
                        scatter(1 - u, range(0, 4), False)
                        turn_x(p + 1, 1 - u, 1, xta_ready, g * 33 + p + 2)
                        pe.wait_ge(h_ready, g * 32 + p + 1)
                        pe.wait_ge(xtb_ready, g * 33 + p + 2)
                        for j in range(2):
                            last = pe.transpose(bank[7][:, j * 128:(j + 1) * 128], mo["h"][:, j * 128:(j + 1) * 128], ident)
                        last.then_inc(ht_done, 1)
                        scatter(1 - u, range(4, 6), False)
                        pe.wait_ge(ht_ready, g * 32 + p + 1)
                        pe.wait_ge(slot_in[base + 2], arrived[2])
                        w = ring[:, base + 2, :].rearrange("p (e j n) -> p e j n", e=2, j=2)
                        for half in range(2):
                            pe.wait_ge(y_ready, g * 64 + p * 2 + half)
                            for j in range(2):
                                for e in range(2):
                                    last = mm(bank[6][64 * e:64 * e + 64, :],
                                              mo["h2"][:, j * 128 + 64 * e:j * 128 + 64 * e + 64],
                                              w[:, e, j, half * 512:(half + 1) * 512], start=(j == 0), stop=(j == 1))
                            last.then_inc(y_done, 1)
                            if half == 0:
                                scatter(1 - u, range(6, 8), True)
                        slot_rows(p + 2, ht_ready, g * 32 + p + 1)
                pe.wait_ge(y_ready, g * 64 + 64)
                pe.wait_ge(selg_ready, g * 33 + 33)
                scatter(1, range(0, 8), True, stop=True)
                pe.reg_add(rounds_run, rounds_run, 1)

            with pe.Fori(0, DEPTH) as l:
                pe.wait_ge(hT_act, l * 6 + 3)
                pe.wait_ge(hT_dve, l * 4 + 2)

                def evacuated(b):
                    if b >= 10 or b % 2 == 0:
                        pe.wait_ge(proj_act, l * 17 + (b // 2 + 1 if b < 10 else b - 4))
                    else:
                        pe.wait_ge(proj_dve, l * 5 + b // 2 + 1)

                def project(b):
                    n = next(i for i, dd in enumerate(DOUBLES) if b in dd[2])
                    c0, c1, blocks = DOUBLES[n]
                    s = DOUBLE_SLOT[n]
                    if b == blocks[0]:
                        pe.wait_ge(slot_in[s], l * (16 * SLOT_LOADS[s]) + 16 * (2 if s == 2 else 1))
                    if b >= 4:
                        evacuated(b - 4)
                    w = slot(s, 0, KC * (c1 - c0)).rearrange("p (k n) -> p k n", k=KC)
                    at, width = BLOCKS[b][0] - c0, BLOCKS[b][1]
                    for kk in range(KC):
                        last = mm(bank[b % 4][0:width, 0:T], w[:, kk, at:at + width], hT[:, kk, :],
                                  start=(kk == 0), stop=(kk == KC - 1))
                    last.then_inc(proj_done, 1)

                for b in range(5):
                    project(b)
                pe.wait_ge(small_mix, l * 64 + 64)
                for h in range(A_HEADS):
                    if h % 2 == 0:
                        evacuated(h // 2)
                    if h >= 4:
                        pe.wait_ge((lat_act, lat_dve)[h % 2], l * 4 + (h - 4) // 2 + 1)
                    r = 64 * (h % 2)
                    mm(bank[4 + h % 4][:, 0:T], wuk[r:r + 64, h // 2, :], qaT[r:r + 64, h // 2, :],
                       start=True, stop=True).then_inc(lat_done, 1)
                for b in range(5, 8):
                    project(b)
                pe.wait_ge(proj_act, l * 17 + 3)
                pe.wait_ge(lat_act, l * 4 + 3)
                for n, (t0, w) in enumerate(CHUNKS):
                    last = pe.transpose(bank[4][0:w, n * 128:(n + 1) * 128], stage[:, 4 % STAGES, t0:t0 + w], ident)
                last.then_inc(ckv_turned, 1)
                for b in range(8, 10):
                    project(b)
                evacuated(9)
                pe.wait_ge(lat_dve, l * 4 + 3)
                for n in (1, 2):
                    t0, w = CHUNKS[n]
                    last = pe.transpose(bank[5][0:w, n * 72:(n + 1) * 72], kwT[0:72, t0:t0 + w], ident[0:72, 0:72])
                last.then_inc(wi_turned, 1)
                pe.wait_ge(ckv_ready, l * 3 + 3)
                hold_here(pe, lat_act, l * 4 + 4)
                for n, (t0, w) in enumerate(CHUNKS):
                    last = pe.transpose(bank[6][:, t0:t0 + w], ckv[0:w, n, :], ident[0:w, 0:w])
                last.then_inc(ckvT_done, 1)

                def index_scores(n, first):
                    t0, w = CHUNKS[n]
                    for h in range(I_HEADS):
                        m = first + h
                        if m == 0:
                            pe.wait_ge(wi_ready, l + 1)
                            pe.wait_ge(ckvT_ready, l + 1)
                            pe.wait_ge(lat_dve, l * 4 + 4)
                            evacuated(5)
                            evacuated(7)
                            evacuated(8)
                        if m >= 4:
                            pe.wait_ge(index_relu, l * 16 + m - 3)
                        r = 64 * (h % 2)
                        keys = kdT if h % 2 else kwT
                        mm(bank[4 + m % 4][:, 0:KEYS[n]], qiT[r:r + 64, h // 2, t0:t0 + w], keys[r:r + 64, 0:KEYS[n]],
                           start=True, stop=True).then_inc(index_done, 1)

                index_scores(2, 0)
                project(10)
                project(11)
                index_scores(1, 8)
                for b in range(12, 15):
                    project(b)

                def turn_group(j0, b0):
                    evacuated(b0 + 3)
                    for n, (t0, w) in enumerate(CHUNKS):
                        j = j0 + n
                        if j == 0:
                            pe.wait_ge(index_relu, l * 16 + 16)
                        if j >= 4:
                            pe.wait_ge(tok_copied, l * 12 + j - 3)
                        for c in range(4):
                            last = pe.transpose(bank[4 + j % 4][0:w, c * 128:(c + 1) * 128],
                                                stage[:, (b0 + c) % STAGES, t0:t0 + w], ident)
                        last.then_inc(tok_turned, 1)

                turn_group(0, 10)
                for b in range(15, 19):
                    project(b)
                turn_group(3, 14)
                for b in range(19, 22):
                    project(b)
                turn_group(6, 18)
                for n, (t0, w) in enumerate(CHUNKS):
                    j = 9 + n
                    pe.wait_ge(tok_copied, l * 12 + j - 3)
                    hold_here(pe, rot_ready, l * 3 + n + 1)
                    for c in range(4):
                        last = pe.transpose(bank[4 + j % 4][:, c * w:(c + 1) * w], rot[0:w, n, c * 128:(c + 1) * 128],
                                            ident[0:w, 0:w])
                    last.then_inc(tok_turned, 1)

                pe.wait_ge(tok_copied, l * 12 + 12)
                hold_here(pe, proj_act, l * 17 + 17)

                def ret_score(h):
                    r, c, b = 64 * (h % 2), h // 2, 2 * (h % 2)
                    if h >= 2:
                        hold_here(pe, ret_decayed, l * 12 + 3 * (h - 1))
                    mm(bank[b][0:16, 0:T], qkT[r:r + 64, 2 + c, 0:16], qkT[r:r + 64, c, 0:T],
                       start=True, stop=True).then_inc(ret_scores, 1)
                    mm(bank[b + 1][:, 0:256], qkT[r:r + 64, 2 + c, 16:144], qkT[r:r + 64, c, 16:T], start=True, stop=True)
                    mm(bank[b + 1][:, 256:384], qkT[r:r + 64, 2 + c, 144:T], qkT[r:r + 64, c, 144:T],
                       start=True, stop=True).then_inc(ret_scores, 1)

                def ret_value(h):
                    hold_here(pe, ret_decayed, l * 12 + 3 * (h + 1))
                    dec = decayed[:, h % 2, :]
                    vs = slice(h * 128, (h + 1) * 128)
                    for n, (t0, w) in enumerate(CHUNKS):
                        parts = [(dec[0:16, t0:t0 + w], v_tok[0:16, 0, vs])]
                        if n >= 1:
                            parts.append((dec[:, T + t0 - 16:T + t0 - 16 + w], v_tok[:, 1, vs]))
                        if n == 2:
                            parts.append((dec[:, T + 256:T + 384], v_tok[:, 2, vs]))
                        for m, (s, v) in enumerate(parts):
                            last = mm(bank[4 + n][0:w, vs], s, v, start=(m == 0), stop=(m == n))
                    last.then_inc(ret_out, 1)

                for h in range(R_HEADS):
                    ret_score(h)
                    if h:
                        ret_value(h - 1)
                ret_value(R_HEADS - 1)

                jobs = [(0, None)] + [(2, h) for h in range(8)] + [(1, h) for h in range(8)]

                def logits(m):
                    n, h = jobs[m]
                    if m >= 4:
                        pe.wait_ge(logits_masked, l * 17 + m - 3)
                    elif m == 0:
                        pe.wait_ge(ret_decayed, l * 12 + 12)
                    t0, w = CHUNKS[n]
                    if m == 0:
                        pe.wait_ge(q0_ready, l + 1)
                    q = work[:, 0:128] if n == 0 else latT[:, h, t0:t0 + w]
                    mm(bank[m % 4][:, 0:KEYS[n]], q, ckvT[:, 0:KEYS[n]], start=True, stop=True).then_inc(logits_done, 1)

                def turn_probs(m):
                    n, _ = jobs[m]
                    pe.wait_ge(prob_ready, l * 17 + m + 1)
                    if m >= 2:
                        pe.wait_ge(prob_copied, l * 17 + m - 1)
                    else:
                        pe.wait_ge(ret_ready, l * 3 + 3)
                    for j in range(n + 1):
                        t0, w = CHUNKS[j]
                        last = pe.transpose(bank[4 + m % 2][0:w, j * 128:(j + 1) * 128], logit[:, m % 4, t0:t0 + w], ident)
                    last.then_inc(prob_turned, 1)

                def out_latent(m):
                    n, h = jobs[m]
                    pe.wait_ge(prob_copied, l * 17 + m + 1)
                    group = (m + 3) // 4
                    if group >= 2 and (m - 1) % 4 == 0:
                        pe.wait_ge(olat_ready, l * 5 + group - 1)
                    c = 0 if m == 0 else (m - 1) % 4 * 128
                    for j in range(n + 1):
                        w = CHUNKS[j][1]
                        last = mm(bank[7 - group % 2][:, c:c + 128], ckv[0:w, j, :], pT[0:w, m % 4, j, :],
                                  start=(j == 0), stop=(j == n))
                    last.then_inc(olat_done, 1)

                for m in range(17 + 4):
                    if m < 17:
                        logits(m)
                    if 0 <= m - 3 < 17:
                        turn_probs(m - 3)
                    if m >= 4:
                        out_latent(m - 4)

                for h in range(A_HEADS):
                    if h == 0:
                        pe.wait_ge(olat_ready, l * 5 + 5)
                    r = 64 * (h % 2)
                    last = mm(bank[h // 2][r:r + 64, 0:T], wuv[:, h, :], latT[:, h, :], start=True, stop=True)
                    if h % 2:
                        last.then_inc(out_a_done, 1)
                for n, (t0, w) in enumerate(CHUNKS):
                    for c in range(4):
                        last = pe.transpose(bank[4 + n][:, c * w:(c + 1) * w], o_ret[0:w, n, c * 128:(c + 1) * 128],
                                            ident[0:w, 0:w])
                    last.then_inc(ret_turned, 1)
                pe.wait_ge(out_a_ready, l * 4 + 4)
                pe.wait_ge(ret_mix, l * 3 + 3)
                for s in (3, 4):
                    pe.wait_ge(slot_in[s], l * (16 * SLOT_LOADS[s]) + 32)
                for n, (t0, w) in enumerate(CHUNKS):
                    for half in range(2):
                        for kk in range(KC):
                            wo = ring[:, 3 + kk // 4, :].rearrange("p (k n) -> p k n", k=4)
                            last = mm(bank[2 * n + half][0:w, :], mixT[kk][:, t0:t0 + w],
                                      wo[:, kk % 4, half * 512:(half + 1) * 512], start=(kk == 0), stop=(kk == KC - 1))
                    last.then_inc(sub_done, 1)
                hold_here(pe, ln_ready, l * 6 + 3)
                turn_h()

                pe.wait_ge(hT_act, l * 6 + 6)
                pe.wait_ge(hT_dve, l * 4 + 4)
                pe.wait_ge(small_moe, l * 32 + 32)
                wr3 = wr[:, :].rearrange("p (k e) -> p k e", k=KC)
                for n, (t0, w) in enumerate(CHUNKS):
                    for kk in range(KC):
                        last = mm(bank[6][0:w, n * E:(n + 1) * E], hT[:, kk, t0:t0 + w], wr3[:, kk, :],
                                  start=(kk == 0), stop=(kk == KC - 1))
                last.then_inc(router_done, 1)
                pe.wait_ge(slot_in[5], l * (16 * SLOT_LOADS[5]) + 48)
                for j in range(2):
                    for part in range(2):
                        w = slot(5, 2048 * part, 2048).rearrange("p (k f) -> p k f", k=KC)
                        for kk in range(KC):
                            last = mm(bank[2 * j + part][:, 0:T], w[:, kk, j * 128:(j + 1) * 128], hT[:, kk, :],
                                      start=(kk == 0), stop=(kk == KC - 1))
                    last.then_inc(shared_done, 1)
                hold_here(pe, chosen_ready, l + 1)
                ch = rows3["chosen"]
                for n, (t0, w) in enumerate(CHUNKS):
                    for m in range(n + 1):
                        wm = CHUNKS[m][1]
                        last = mm(bank[5][0:w, n * E:(n + 1) * E], k["before" if m == n else "ones"][0:wm, 0:w],
                                  ch[0:wm, m, :], start=(m == 0), stop=(m == n))
                for m in range(3):
                    wm = CHUNKS[m][1]
                    last = mm(bank[5][:, 3 * E:4 * E], k["ones"][0:wm, :], ch[0:wm, m, :], start=(m == 0), stop=(m == 2))
                last.then_inc(rank_done, 1)
                pe.wait_ge(shared_ready, l * 2 + 2)
                opened = set()
                for d in range(8):
                    for b, c, t, n in acc_segments(d):
                        for j in range(2):
                            last = mm(bank[b][:, c:c + n], slot(2, 2048 + j * 1024 + d * 128, 128), hsT[:, j, t:t + n],
                                      start=b not in opened, stop=False, skip_group_check=True)
                            opened.add(b)
                last.then_inc(shared_down, 1)
                pe.wait_ge(rank_ready, l + 1)
                pe.wait_ge(score_ready, l * 2 + 2)
                round_(l, 0, False)
                hold_here(pe, count_ready, l + 1)
                most = pe.value_load(count_i[0:1, 0:1], min_val=0, max_val=T)
                with pe.If(most > CAP):
                    with pe.Fori(1, ROUNDS) as r:
                        round_(l, r, True)
                with pe.Else():
                    for s, per in ((gates_used, 32), (gu_done, 32), (xta_done, 33), (xtb_done, 33), (ht_done, 32),
                                   (y_done, 64), (scattered, 33), (slot_row_done, 34)):
                        pe.wait_ge(s, l * (ROUNDS * per) + per)
                        pe.sem_inc(s, EXTRA * per)

                pe.wait_ge(acc_act, l * 3 + 3)
                pe.wait_ge(acc_dve, l * 2 + 2)
                for n, (t0, w) in enumerate(CHUNKS):
                    for d in range(8):
                        last = pe.transpose(bank[2 * n + d // 4][0:w, d % 4 * 128:(d % 4 + 1) * 128],
                                            accT[:, d * T + t0:d * T + t0 + w], ident)
                    last.then_inc(sub_done, 1)
                hold_here(pe, ln_ready, l * 6 + 6)
                turn_h()

        @block.scalar
        def _(act):
            def copy(o, i, s):
                act.activation(o, i, ACT.Copy).then_inc(s, 1)

            def h_feature(base):
                for j, (n, at) in enumerate(((0, 1), (1, 2), (2, 4))):
                    t0, w = CHUNKS[n]
                    act.wait_ge(hT_turned, base * 5 + at)
                    kk = KC if n == 0 else 4
                    copy(hT[:, 0:kk, t0:t0 + w], bank[2 * n][:, 0:kk * w].rearrange("p (k t) -> p k t", k=kk), hT_act)

            act.wait_ge(const_in, 16)
            h_feature(0)

            def layer_norm(l, ph):
                for n, (t0, w) in enumerate(CHUNKS):
                    act.wait_ge(ln_shift_ready, l * 6 + ph * 3 + n + 1)
                    act.wait_ge(ln_rstd_ready, l * 6 + ph * 3 + n + 1)
                    act.activation(h_tok[0:w, n, :], h_tok[0:w, n, :], ACT.Identity, bias=ln_shift[0:w, n:n + 1],
                                   scale=ln_rstd[0:w, n:n + 1]).then_inc(ln_norm, 1)

            def round_(l, r):
                g = l * ROUNDS + r
                def turned(q, u):
                    act.wait_ge(xta_done, g * 33 + q + 1)
                    act.activation(xgT[:, u, 0:4, :], bank[7][:, :].rearrange("p (k s) -> p k s", k=4), ACT.Copy)\
                        .then_inc(xta_ready, 1)

                turned(0, 0)
                with act.Fori(0, PAIRS // 2) as i:
                    for u in range(2):
                        p = i * 2 + u
                        act.wait_ge(ha_ready, g * 32 + p)
                        act.wait_ge(gu_done, g * 32 + p + 1)
                        act.activation(mo["sg"], bank[5][:, 0:F], ACT.Sigmoid).then_inc(sig_ready, 1)
                        turned(p + 1, 1 - u)
                        act.wait_ge(scattered, g * 33 + p)
                        for half in range(2):
                            act.wait_ge(y_done, g * 64 + p * 2 + half + 1)
                            act.activation(y_sb[:, u, half * 512:(half + 1) * 512], bank[6][:, :], ACT.Copy)\
                                .then_inc(y_ready, 1)

            with act.Fori(0, DEPTH) as l:
                def proj(b):
                    act.wait_ge(proj_done, l * 22 + b + 1)
                    if b == 16:
                        act.wait_ge(tok_turned, l * 12 + 3)
                    if b == 20:
                        act.wait_ge(tok_turned, l * 12 + 6)
                    if b < 4:
                        dst = qaT[:, b, :]
                    elif b in (6, 8):
                        dst = qiT[:, b - 5, :]
                    else:
                        dst = stage[:, b % STAGES, :]
                    copy(dst, bank[b % 4][:, 0:T], proj_act)

                for b in (0, 2, 4):
                    proj(b)
                for h in (0, 2, 4, 6):
                    act.wait_ge(lat_done, l * 8 + h + 1)
                    copy(latT[:, h, :], bank[4 + h % 4][:, 0:T], lat_act)
                proj(6)
                act.wait_ge(ckv_turned, l + 1)
                for n, (t0, w) in enumerate(CHUNKS):
                    if n:
                        act.wait_ge(ckv_ssq, l * 3 + n)
                    act.activation(rl[0:w, 0, 0:128], bank[4][0:w, n * 128:(n + 1) * 128], ACT.Square,
                                   accum_out=ssq[0:w, n:n + 1]).then_inc(ckv_ssq, 1)
                proj(8)
                act.wait_ge(ckv_ssq, l * 3 + 3)

                def relu(n, first):
                    for h in range(I_HEADS):
                        m = first + h
                        act.wait_ge(index_done, l * 16 + m + 1)
                        if m >= 2:
                            act.wait_ge(index_added, l * 16 + m - 1)
                        act.activation(rl[:, m % 2, 0:KEYS[n]], bank[4 + m % 4][:, 0:KEYS[n]], ACT.Relu)\
                            .then_inc(index_relu, 1)

                relu(2, 0)
                proj(10)
                proj(11)
                relu(1, 8)
                for b in range(12, 15):
                    proj(b)

                def token_major(j0, dst):
                    for n, (t0, w) in enumerate(CHUNKS):
                        act.wait_ge(tok_turned, l * 12 + j0 + n + 1)
                        copy(dst[0:w, n, :], bank[4 + (j0 + n) % 4][0:w, :], tok_copied)

                token_major(0, rot)
                for b in range(15, 19):
                    proj(b)
                token_major(3, v_tok)
                for b in range(19, 22):
                    proj(b)
                act.wait_ge(index_added, l * 16 + 16)
                for n, (t0, w) in enumerate(CHUNKS):
                    act.wait_ge(tok_turned, l * 12 + 7 + n)
                    if n:
                        act.wait_ge(gate_mul, l * 3 + n)
                    act.activation(sg_tmp[0:w, :], bank[4 + (6 + n) % 4][0:w, :], ACT.Sigmoid).then_inc(gate_sig, 1)
                    copy(gate[0:w, n, :], bank[4 + (6 + n) % 4][0:w, :], tok_copied)
                for n, (t0, w) in enumerate(CHUNKS):
                    j = 9 + n
                    act.wait_ge(tok_turned, l * 12 + j + 1)
                    copy(qkT[:, :, t0:t0 + w], bank[4 + j % 4][:, 0:4 * w].rearrange("p (c t) -> p c t", c=4), tok_copied)

                def probs(m):
                    n = 0 if m == 0 else (2 if m < 9 else 1)
                    act.wait_ge(prob_turned, l * 17 + m + 1)
                    if m >= 4:
                        act.wait_ge(olat_done, l * 17 + m - 3)
                    b = bank[4 + m % 2]
                    first = act.activation(pT[0:16, m % 4, 0, :], b[0:16, 0:128], ACT.Copy)
                    if n == 0:
                        first.then_inc(prob_copied, 1)
                    else:
                        act.activation(pT[:, m % 4, 1:n + 1, :], b[:, 128:(n + 1) * 128].rearrange("p (j q) -> p j q", j=n),
                                       ACT.Copy).then_inc(prob_copied, 1)

                for m in range(17 + 2):
                    if m < 17:
                        n = 0 if m == 0 else (2 if m < 9 else 1)
                        act.wait_ge(max_ready, l * 17 + m + 1)
                        x = logit[:, m % 4, 0:KEYS[n]]
                        act.activation(x, x, ACT.Exp, bias=neg_max[:, m:m + 1], scale=A_DIM ** -0.5,
                                       accum_out=row_sum[:, m:m + 1]).then_inc(exp_done, 1)
                    if m >= 2:
                        probs(m - 2)
                for b in (0, 2):
                    act.wait_ge(out_a_done, l * 4 + b + 1)
                    if b:
                        act.wait_ge(out_a_ready, l * 4 + 2)
                    act.activation(mixT[b], bank[b][:, 0:T], ACT.Copy).then_inc(out_a_ready, 1)
                for n, (t0, w) in enumerate(CHUNKS):
                    act.wait_ge(ret_turned, l * 3 + n + 1)
                    copy(qkT[:, :, t0:t0 + w], bank[4 + n][:, 0:4 * w].rearrange("p (c t) -> p c t", c=4), ret_mix)
                layer_norm(l, 0)
                h_feature(2 * l + 1)
                act.dma_start(h_rows[0:META, :], h_tok[0:META, 0, :]).then_inc(h_stored, 16)
                act.dma_start(h_rows[META:T, :].rearrange("(c p) d -> p c d", p=128), h_tok[:, 1:3, :]).then_inc(h_stored, 16)

                act.wait_ge(router_done, l + 1)
                act.wait_ge(moe_clear, l * 3 + 3)
                act.activation(rows3["score"][0:16, 0, :], bank[6][0:16, 0:E], ACT.Sigmoid).then_inc(score_ready, 1)
                act.activation(rows3["score"][:, 1:3, :], bank[6][:, E:3 * E].rearrange("p (c e) -> p c e", c=2),
                               ACT.Sigmoid).then_inc(score_ready, 1)
                for j in range(2):
                    act.wait_ge(shared_done, l * 2 + j + 1)
                    act.activation(sgs[:, j, :], bank[2 * j][:, 0:T], ACT.Sigmoid).then_inc(shared_sig, 1)
                round_(l, 0)
                hold_here(act, count_ready, l + 1)
                most = act.value_load(count_i[0:1, 0:1], min_val=0, max_val=T)
                with act.If(most > CAP):
                    with act.Fori(1, ROUNDS) as r:
                        round_(l, r)
                with act.Else():
                    for s, per in ((sig_ready, 32), (xta_ready, 33), (y_ready, 64)):
                        act.wait_ge(s, l * (ROUNDS * per) + per)
                        act.sem_inc(s, EXTRA * per)
                act.wait_ge(scattered, l * (33 * ROUNDS) + 33 * ROUNDS)
                for b in (0, 2, 4):
                    n = min(512, 8 * T - b * 512)
                    copy(accT[:, b * 512:b * 512 + n], bank[b][:, 0:n], acc_act)
                layer_norm(l, 1)
                h_feature(2 * l + 2)

        @block.vector
        def _(dve):
            steps = [0]

            def step(ins):
                steps[0] += 1
                ins.then_inc(dve_step, 1)

            def after_steps():
                dve.wait_ge(dve_step, steps[0])

            def h_feature(base):
                for j, (n, at) in enumerate(((1, 3), (2, 5))):
                    t0, w = CHUNKS[n]
                    dve.wait_ge(hT_turned, base * 5 + at)
                    dve.tensor_copy(hT[:, 4:8, t0:t0 + w], bank[2 * n + 1][:, 0:4 * w].rearrange("p (k t) -> p k t", k=4))\
                        .then_inc(hT_dve, 1)

            dve.memset(ssq[:], 1.0).then_inc(dve_step, 1)
            dve.memset(ret_mv[:], 1.0).then_inc(dve_step, 1)
            dve.wait_ge(dve_step, 2)
            dve.wait_ge(const_in, 16)
            h_feature(0)

            def layer_norm(l, ph):
                base = l * 6 + ph * 3

                def residual(n):
                    w = CHUNKS[n][1]
                    dve.wait_ge(sub_done, base + n + 1)
                    for half in range(2):
                        hs_ = slice(half * 512, (half + 1) * 512)
                        dve.scalar_tensor_tensor(h_tok[0:w, n, hs_], h_tok[0:w, n, hs_], ALPHA, bank[2 * n + half][0:w, :],
                                                 ALU.mult, ALU.add).then_inc(z_ready, 1)
                    for half in range(2):
                        dve.wait_ge(z_ready, 2 * base + 2 * n + half + 1)
                        step(dve.bn_stats(ln_stats[0:w, n, 6 * half:6 * half + 6],
                                          h_tok[0:w, n, half * 512:(half + 1) * 512]))
                    after_steps()
                    step(dve.bn_aggr(ln_mv[0:w, n, :], ln_stats[0:w, n, :]))
                    after_steps()
                    dve.tensor_scalar(ln_var[0:w, n:n + 1], ln_mv[0:w, n, 1:2], EPS, None, ALU.add).then_inc(ln_var_ready, 1)

                def shift(n):
                    w = CHUNKS[n][1]
                    dve.wait_ge(ln_rstd_ready, base + n + 1)
                    dve.scalar_tensor_tensor(ln_shift[0:w, n:n + 1], ln_mv[0:w, n, 0:1], -1.0, ln_rstd[0:w, n:n + 1],
                                             ALU.mult, ALU.mult).then_inc(ln_shift_ready, 1)

                def scale(n):
                    w = CHUNKS[n][1]
                    dve.wait_ge(ln_norm, base + n + 1)
                    dve.tensor_tensor(h_tok[0:w, n, :], h_tok[0:w, n, :], ln_par[0:w, 0, :], ALU.mult).then_inc(ln_scaled, 1)

                residual(0)
                residual(1)
                shift(0)
                residual(2)
                shift(1)
                dve.wait_ge(ln_par_in, l * 64 + ph * 32 + 32)
                scale(0)
                shift(2)
                scale(1)
                scale(2)

            def round_(l, r, extra):
                g = l * ROUNDS + r
                def select(q):
                    dve.wait_ge(slot_row_done, g * 34 + q)
                    at = q * 6
                    dve.tensor_copy(mo["pb"].rearrange("p (c n) -> p c n", c=3),
                                    route_pairs[:, :, bass.ds(at, 6)]).then_inc(pair_ready, 1)
                    dve.wait_ge(pair_ready, g * 34 + q + 1)
                    dve.tensor_tensor(sel.rearrange("p c e s -> p (c e) s"),
                                      k["iota"].unsqueeze(1).to_broadcast([128, 6, CAP]),
                                      pb.rearrange("p c e v -> p (c e) v")[:, :, 2:3].to_broadcast([128, 6, CAP]),
                                      ALU.is_equal).then_inc(sel_ready, 1)

                def slot_rows(q, u):
                    dve.wait_ge(slot_row_done, g * 34 + q + 1)
                    dve.tensor_copy(idg[:, u, :], bank[7][:, 0:2]).then_inc(idg_ready, 1)
                    dve.tensor_scalar(rank_i[:, u:u + 1], bank[7][:, 0:1], FAR, None, ALU.add).then_inc(slot_row_ready, 1)

                def turned(q, u):
                    dve.wait_ge(xtb_done, g * 33 + q + 1)
                    dve.tensor_copy(xgT[:, u, 4:8, :], bank[7][:, :].rearrange("p (k s) -> p k s", k=4)).then_inc(xtb_ready, 1)

                if extra:
                    dve.wait_ge(slot_row_done, g * 34)
                    dve.tensor_scalar(route[:, :, :, 2], route[:, :, :, 2], -float(CAP), None, ALU.add).then_inc(shifted, 1)
                    dve.wait_ge(shifted, l * EXTRA + r)
                dve.wait_ge(scattered, g * 33)
                dve.memset(selg[:, 1, :], 0.0).then_inc(selg_ready, 1)
                for q in range(2):
                    select(q)
                    slot_rows(q, q)
                turned(0, 0)
                with dve.Fori(0, PAIRS // 2) as i:
                    for u in range(2):
                        p = i * 2 + u
                        select(p + 2)
                        dve.wait_ge(idg_ready, g * 34 + p + 1)
                        dve.wait_ge(scattered, g * 33 + p)
                        dve.tensor_scalar(selg[:, u, :], k["iota_t"], idg[:, u, 0:1], idg[:, u, 1:2],
                                          ALU.is_equal, ALU.mult).then_inc(selg_ready, 1)
                        dve.wait_ge(sig_ready, g * 32 + p + 1)
                        dve.tensor_tensor(mo["ha"], mo["sg"], bank[5][:, 0:F], ALU.mult).then_inc(ha_ready, 1)
                        dve.wait_ge(gu_done, g * 32 + p + 1)
                        dve.wait_ge(ht_done, g * 32 + p)
                        dve.wait_ge(ha_ready, g * 32 + p + 1)
                        dve.tensor_tensor(mo["h"], mo["ha"], bank[5][:, F:2 * F], ALU.mult).then_inc(h_ready, 1)
                        turned(p + 1, 1 - u)
                        dve.wait_ge(ht_done, g * 32 + p + 1)
                        dve.tensor_copy(mo["h2"], bank[7][:, 0:F]).then_inc(ht_ready, 1)
                        slot_rows(p + 2, u)

            with dve.Fori(0, DEPTH) as l:
                steps[0] = 0
                dve.sem_clear(dve_step)

                def proj(b):
                    dve.wait_ge(proj_done, l * 22 + b + 1)
                    dst = qaT[:, b, :] if b < 4 else qiT[:, b - 5, :]
                    dve.tensor_copy(dst, bank[b % 4][:, 0:T]).then_inc(proj_dve, 1)

                proj(1)
                proj(3)
                for h in (1, 3, 5, 7):
                    dve.wait_ge(lat_done, l * 8 + h + 1)
                    dve.tensor_copy(latT[:, h, :], bank[4 + h % 4][:, 0:T]).then_inc(lat_dve, 1)
                proj(5)
                proj(7)
                dve.wait_ge(ckv_ssq, l * 3 + 3)
                dve.tensor_scalar(ckv_var[:, :], ssq[:, :], 1.0 / LAT, EPS, ALU.mult, ALU.add).then_inc(ckv_var_ready, 1)
                dve.wait_ge(small_mix, l * 64 + 64)
                dve.wait_ge(ckv_rstd_ready, l + 1)
                for n, (t0, w) in enumerate(CHUNKS):
                    dve.scalar_tensor_tensor(ckv[0:w, n, :], bank[4][0:w, n * 128:(n + 1) * 128], ckv_rstd[0:w, n:n + 1],
                                             kvn_w[0:w, :], ALU.mult, ALU.mult).then_inc(ckv_ready, 1)
                dve.wait_ge(proj_done, l * 22 + 10)
                step(dve.tensor_copy(kdT[64:128, :], bank[1][0:64, 0:T]))
                dve.tensor_copy(kwT[0:72, :], bank[1][0:72, 0:T]).then_inc(proj_dve, 1)
                dve.wait_ge(wi_turned, l + 1)
                dve.tensor_scalar(wi[:, 1:3, :], bank[5][:, 72:216].rearrange("p (c n) -> p c n", c=2)[:, :, 64:72],
                                  I_HEADS ** -0.5, None, ALU.mult).then_inc(wi_ready, 1)
                dve.wait_ge(ckvT_done, l + 1)
                dve.tensor_copy(ckvT, bank[6][:, 0:T]).then_inc(ckvT_ready, 1)

                def choose(n, first):
                    K = KEYS[n]
                    wk = work[:, 0:K]
                    for h in range(I_HEADS):
                        m = first + h
                        dve.wait_ge(index_relu, l * 16 + m + 1)
                        dve.wait_ge(wi_ready if h == 0 else index_added, l + 1 if h == 0 else l * 16 + m)
                        dve.scalar_tensor_tensor(wk, rl[:, m % 2, 0:K], wi[:, n, h:h + 1], causal[n] if h == 0 else wk,
                                                 ALU.mult, ALU.add).then_inc(index_added, 1)
                    hold_here(dve, index_added, l * 16 + first + 8)
                    for _ in range(N_SEL // 8):
                        step(dve.max(best8[:, :], wk))
                        after_steps()
                        step(dve.match_replace(wk, best8[:, :], wk, TAKEN))
                        after_steps()
                    step(dve.tensor_scalar(masks[n], wk, -2e38, NEG, ALU.is_gt, ALU.mult))
                    after_steps()
                    step(dve.tensor_tensor(masks[n], masks[n], causal[n], ALU.min))
                    after_steps()

                choose(2, 0)
                choose(1, 8)
                dve.wait_ge(lat_act, l * 4 + 4)
                dve.wait_ge(lat_dve, l * 4 + 4)
                dve.tensor_copy(work[:, 0:128].rearrange("p (h q) -> p h q", h=8), latT[:, :, 0:16]).then_inc(q0_ready, 1)

                for h in range(R_HEADS):
                    b = 2 * (h % 2)
                    dve.wait_ge(ret_scores, l * 8 + 2 * h + 2)
                    if h >= 2:
                        dve.wait_ge(ret_out, l * 4 + h - 1)
                    dec = decayed[:, h % 2, :]
                    dve.tensor_tensor(dec[0:16, 0:T], bank[b][0:16, 0:T], decay[0:16, h, :], ALU.mult).then_inc(ret_decayed, 1)
                    dve.tensor_tensor(dec[:, T:T + 256], bank[b + 1][:, 0:256], decay[:, h, 0:256], ALU.mult)\
                        .then_inc(ret_decayed, 1)
                    dve.tensor_tensor(dec[:, T + 256:T + 384], bank[b + 1][:, 256:384], decay[:, h, 0:128], ALU.mult)\
                        .then_inc(ret_decayed, 1)
                dve.wait_ge(ret_out, l * 4 + 4)
                for n, (t0, w) in enumerate(CHUNKS):
                    for h in range(R_HEADS):
                        step(dve.bn_stats(ret_stats[0:w, 4 * n + h, :], bank[4 + n][0:w, h * 128:(h + 1) * 128]))
                after_steps()
                for n, (t0, w) in enumerate(CHUNKS):
                    for h in range(R_HEADS):
                        step(dve.bn_aggr(ret_mv[0:w, 4 * n + h, :], ret_stats[0:w, 4 * n + h, :]))
                after_steps()
                dve.tensor_scalar(ret_var[:, :], ret_mv[:, :, 1], EPS, None, ALU.add).then_inc(ret_var_ready, 1)
                dve.wait_ge(ret_rstd_ready, l + 1)
                for n, (t0, w) in enumerate(CHUNKS):
                    for h in range(R_HEADS):
                        c = 4 * n + h
                        step(dve.tensor_scalar(o_ret[0:w, n, h * 128:(h + 1) * 128], bank[4 + n][0:w, h * 128:(h + 1) * 128],
                                               ret_mv[0:w, c, 0:1], ret_rstd[0:w, c:c + 1], ALU.subtract, ALU.mult))
                dve.wait_ge(gate_ready, l * 3 + 3)
                after_steps()
                for n, (t0, w) in enumerate(CHUNKS):
                    dve.tensor_tensor(o_ret[0:w, n, :], o_ret[0:w, n, :], gate[0:w, n, :], ALU.mult).then_inc(ret_ready, 1)

                for m in range(17 + 4):
                    if m < 17:
                        n = 0 if m == 0 else (2 if m < 9 else 1)
                        hold_here(dve, logits_done, l * 17 + m + 1)
                        if m >= 4:
                            hold_here(dve, prob_turned, l * 17 + m - 3)
                        K = KEYS[n]
                        dve.tensor_tensor_reduce(logit[:, m % 4, 0:K], bank[m % 4][:, 0:K],
                                                 k["causal0"] if n == 0 else masks[n], 1.0, -3e38, ALU.add, ALU.max,
                                                 row_max[:, m:m + 1]).then_inc(logits_masked, 1)
                        dve.wait_ge(logits_masked, l * 17 + m + 1)
                        dve.tensor_scalar(neg_max[:, m:m + 1], row_max[:, m:m + 1], -(A_DIM ** -0.5), None, ALU.mult)\
                            .then_inc(max_ready, 1)
                    if 1 <= m <= 17:
                        dve.wait_ge(exp_done, l * 17 + m)
                        dve.reciprocal(row_inv[:, m - 1:m], row_sum[:, m - 1:m]).then_inc(inv_ready, 1)
                    if m >= 4 and (m - 4) % 4 == 0:
                        grp = (m - 4) // 4
                        dve.wait_ge(olat_done, l * 17 + 4 * grp + 1)
                        if grp == 0:
                            o, i_ = latT[:, :, 0:16], bank[7][:, 0:128].rearrange("p (h q) -> p h q", h=8)
                        else:
                            t0 = CHUNKS[2 if grp <= 2 else 1][0]
                            h0 = 4 * ((grp - 1) % 2)
                            o = latT[:, h0:h0 + 4, t0:t0 + 128]
                            i_ = bank[7 - grp % 2][:, :].rearrange("p (h q) -> p h q", h=4)
                        dve.tensor_copy(o, i_).then_inc(olat_ready, 1)
                for b in (1, 3):
                    dve.wait_ge(out_a_done, l * 4 + b + 1)
                    dve.wait_ge(out_a_ready, l * 4 + b)
                    dve.tensor_copy(mixT[b], bank[b][:, 0:T]).then_inc(out_a_ready, 1)
                layer_norm(l, 0)
                h_feature(2 * l + 1)

                s3 = rows3
                dve.wait_ge(score_ready, l * 2 + 2)
                dve.wait_ge(small_moe, l * 32 + 32)
                step(dve.tensor_tensor(s3["biased"], s3["score"], rbias[:, :].unsqueeze(1).to_broadcast([128, 3, E]), ALU.add))
                after_steps()
                for n in range(3):
                    for gr in range(GROUPS):
                        step(dve.max(cube["best2"][:, n, gr, :], cube["biased"][:, n, gr, :]))
                after_steps()
                step(dve.tensor_tensor(s3["grp"], cube["best2"][:, :, :, 0], cube["best2"][:, :, :, 1], ALU.add))
                after_steps()
                other = s3["grp"].unsqueeze(2).to_broadcast([128, 3, 8, 8])
                own = s3["grp"].unsqueeze(3).to_broadcast([128, 3, 8, 8])
                step(dve.tensor_tensor(cube["gt"], other, own, ALU.is_gt))
                step(dve.tensor_tensor(cube["eq"], other, own, ALU.is_equal))
                after_steps()
                step(dve.tensor_tensor(mo["eq"].rearrange("p (c n) -> p c n", c=3), mo["eq"].rearrange("p (c n) -> p c n", c=3),
                                       k["tri"].unsqueeze(1).to_broadcast([128, 3, 64]), ALU.mult))
                after_steps()
                step(dve.tensor_tensor(mo["gt"], mo["gt"], mo["eq"], ALU.add))
                after_steps()
                step(dve.tensor_reduce(s3["rank"], cube["gt"], AX, ALU.add))
                after_steps()
                step(dve.tensor_scalar(mo["rank"], mo["rank"], TOP_GROUPS - 0.5, NEG, ALU.is_gt, ALU.mult))
                after_steps()
                step(dve.tensor_tensor(cube["biased"], cube["biased"], s3["rank"].unsqueeze(3).to_broadcast([128, 3, 8, 8]),
                                       ALU.add))
                after_steps()
                for n in range(3):
                    step(dve.max(best8[:, :], s3["biased"][:, n, :]))
                    after_steps()
                    step(dve.match_replace(s3["picked"][:, n, :], best8[:, :], s3["biased"][:, n, :], TAKEN))
                    after_steps()
                dve.tensor_scalar(mo["chosen"], mo["picked"], -2e38, None, ALU.is_le).then_inc(chosen_ready, 1)
                dve.wait_ge(chosen_ready, l + 1)
                step(dve.tensor_tensor(mo["tmp"], mo["score"], mo["chosen"], ALU.mult))
                after_steps()
                step(dve.tensor_reduce(mo["gsum"], s3["tmp"], AX, ALU.add))
                after_steps()
                step(dve.reciprocal(mo["ginv"], mo["gsum"]))
                dve.wait_ge(moe_coded, l + 1)
                after_steps()
                dve.scalar_tensor_tensor(route[:, :, 0:E, 1], s3["tmp"], ROUTE_SCALE,
                                         mo["ginv"].unsqueeze(2).to_broadcast([128, 3, E]), ALU.mult, ALU.mult)\
                    .then_inc(gates_ready, 1)
                for j in range(2):
                    dve.wait_ge(shared_sig, l * 2 + j + 1)
                    step(dve.tensor_tensor(hs[:, j, :], sgs[:, j, :], bank[2 * j][:, 0:T], ALU.mult))
                    after_steps()
                    dve.tensor_tensor(hsT[:, j, :], hs[:, j, :], bank[2 * j + 1][:, 0:T], ALU.mult).then_inc(shared_ready, 1)
                dve.wait_ge(rank_done, l + 1)
                b5 = bank[5][:, 0:3 * E].rearrange("p (c e) -> p c e", c=3)
                step(dve.scalar_tensor_tensor(s3["tmp"][0:16, 0, :], b5[0:16, 0, :], 1.0, s3["chosen"][0:16, 0, :],
                                              ALU.add, ALU.mult))
                step(dve.scalar_tensor_tensor(s3["tmp"][:, 1:3, :], b5[:, 1:3, :], 1.0, s3["chosen"][:, 1:3, :],
                                              ALU.add, ALU.mult))
                step(dve.tensor_reduce(mo["cmax"][0:1, :], bank[5][0:1, 3 * E:4 * E], AX, ALU.max))
                after_steps()
                step(dve.tensor_scalar(route[0:16, 0, 0:E, 2], s3["tmp"][0:16, 0, :], -1.0, None, ALU.add))
                dve.tensor_scalar(route[:, 1:3, 0:E, 2], s3["tmp"][:, 1:3, :], -1.0, None, ALU.add).then_inc(rank_ready, 1)
                dve.tensor_copy(count_i[0:1, :], mo["cmax"][0:1, :]).then_inc(count_ready, 1)
                after_steps()
                dve.wait_ge(rank_ready, l + 1)
                dve.wait_ge(gates_ready, l + 1)
                round_(l, 0, False)
                hold_here(dve, count_ready, l + 1)
                most = dve.value_load(count_i[0:1, 0:1], min_val=0, max_val=T)
                with dve.If(most > CAP):
                    with dve.Fori(1, ROUNDS) as r:
                        round_(l, r, True)
                with dve.Else():
                    dve.sem_inc(shifted, EXTRA)
                    for s, per in ((selg_ready, 33), (pair_ready, 34), (sel_ready, 34), (ha_ready, 32), (h_ready, 32),
                                   (xtb_ready, 33), (ht_ready, 32), (idg_ready, 34), (slot_row_ready, 34)):
                        dve.wait_ge(s, l * (ROUNDS * per) + per)
                        dve.sem_inc(s, EXTRA * per)
                dve.wait_ge(scattered, l * (33 * ROUNDS) + 33 * ROUNDS)
                for b in (1, 3):
                    dve.tensor_copy(accT[:, b * 512:(b + 1) * 512], bank[b][:, :]).then_inc(acc_dve, 1)
                layer_norm(l, 1)
                h_feature(2 * l + 2)

        @block.gpsimd
        def _(pool):
            steps = [0]

            def step(ins):
                steps[0] += 1
                ins.then_inc(pool_step, 1)

            def after_steps():
                pool.wait_ge(pool_step, steps[0])

            rounds_run = pool.alloc_register("rounds_run")
            pool.reg_mov(rounds_run, 0)
            step(pool.memset(half_pow[:, :], -0.5))
            pool.wait_ge(const_in, 16)
            after_steps()

            def layer_norm(l, ph):
                base = l * 6 + ph * 3
                for n, (t0, w) in enumerate(CHUNKS):
                    pool.wait_ge(ln_var_ready, base + n + 1)
                    pool.tensor_tensor(ln_rstd[0:w, n:n + 1], ln_var[0:w, n:n + 1], half_pow[0:w, 0:1], ALU.pow)\
                        .then_inc(ln_rstd_ready, 1)
                for n, (t0, w) in enumerate(CHUNKS):
                    pool.wait_ge(ln_scaled, base + n + 1)
                    pool.tensor_tensor(h_tok[0:w, n, :], h_tok[0:w, n, :], ln_par[0:w, 1, :], ALU.add).then_inc(ln_ready, 1)

            def load_ln(l, g_, b_):
                for j, src in enumerate((a[g_], a[b_])):
                    pool.dma_start(ln_par[:, j, :], src[bass.ds(l, 1), :].partition_broadcast(128)).then_inc(ln_par_in, 16)

            def round_(l, r, extra):
                g = l * ROUNDS + r
                def gather(q, u):
                    pool.wait_ge(slot_row_ready, g * 34 + q + 1)
                    hold_here(pool, xtb_done, g * 33 + q - 1 if not isinstance(q, int) else g * 33)
                    pool.indirect_dma_start(out=xg[:, u, :], out_offset=None, in_=h_rows,
                                            in_offset=bass.IndirectOffsetOnAxis(ap=rank_i[:, u:u + 1], axis=0),
                                            bounds_check=T - 1, oob_is_err=False).then_inc(gathered[u], 16)

                gather(0, 0)
                gather(1, 1)
                with pool.Fori(0, PAIRS // 2) as i:
                    for u in range(2):
                        gather(i * 2 + (u + 2), u)
                hold_here(pool, gathered[1], pool.snap(rounds_run) * (16 * 17) + 16 * 17)
                pool.reg_add(rounds_run, rounds_run, 1)

            with pool.Fori(0, DEPTH) as l:
                steps[0] = 0
                pool.sem_clear(pool_step)
                pool.dma_start(wuk[:, :, :], a["w_uk"][bass.ds(l, 1)].rearrange("l (j e) d c -> (l e d) j c", e=2))\
                    .then_inc(small_mix, 16)
                pool.dma_start(wuv[:, :, :], a["w_uv"][bass.ds(l, 1)].rearrange("l h c d -> (l c) h d")).then_inc(small_mix, 16)
                pool.dma_start(kvn_w[:, :], a["kv_norm_w"][bass.ds(l, 1), :].partition_broadcast(128)).then_inc(small_mix, 16)
                pool.dma_start(retn_w[:, :], a["ret_norm_w"][bass.ds(l, 1), :].partition_broadcast(128)).then_inc(small_mix, 16)
                pool.dma_start(wr[:, :], a["w_router"][bass.ds(l, 1)].rearrange("l (p k) e -> (l p) (k e)", k=KC))\
                    .then_inc(small_moe, 16)
                pool.dma_start(rbias[:, :], a["router_bias"][bass.ds(l, 1), :].partition_broadcast(128)).then_inc(small_moe, 16)
                load_ln(l, "ln1_g", "ln1_b")
                pool.wait_ge(ckv_var_ready, l + 1)
                pool.tensor_tensor(ckv_rstd[:, :], ckv_var[:, :], half_pow[:, 0:3], ALU.pow).then_inc(ckv_rstd_ready, 1)
                for n, (t0, w) in enumerate(CHUNKS):
                    x = rot[0:w, n, :].rearrange("p (h s f) -> p h s f", h=8, s=2)
                    xa = rot_a[0:w, :].rearrange("p (h s f) -> p h s f", h=8, s=2)
                    xb = rot_b[0:w, :].rearrange("p (h s f) -> p h s f", h=8, s=2)
                    cs = cos3[0:w, n, :].unsqueeze(1).to_broadcast([w, 8, 32])
                    sn = sin3[0:w, n, :].unsqueeze(1).to_broadcast([w, 8, 32])
                    pool.wait_ge(tok_copied, l * 12 + n + 1)
                    for s in range(2):
                        step(pool.tensor_tensor(xa[:, :, s, :], x[:, :, s, :], cs, ALU.mult))
                        step(pool.tensor_tensor(xb[:, :, s, :], x[:, :, 1 - s, :], sn, ALU.mult))
                    after_steps()
                    step(pool.tensor_tensor(x[:, :, 0, :], xa[:, :, 0, :], xb[:, :, 0, :], ALU.subtract))
                    pool.tensor_tensor(x[:, :, 1, :], xa[:, :, 1, :], xb[:, :, 1, :], ALU.add).then_inc(rot_ready, 1)
                    pool.wait_ge(rot_ready, l * 3 + n + 1)
                    after_steps()
                pool.wait_ge(small_mix, l * 64 + 64)
                for n, (t0, w) in enumerate(CHUNKS):
                    pool.wait_ge(gate_sig, l * 3 + n + 1)
                    pool.wait_ge(tok_copied, l * 12 + 7 + n)
                    pool.tensor_tensor(gate[0:w, n, :], gate[0:w, n, :], sg_tmp[0:w, :], ALU.mult).then_inc(gate_mul, 1)
                    pool.wait_ge(gate_mul, l * 3 + n + 1)
                    pool.tensor_tensor(gate[0:w, n, :], gate[0:w, n, :], retn_w[0:w, :], ALU.mult).then_inc(gate_ready, 1)
                pool.wait_ge(ret_var_ready, l + 1)
                pool.tensor_tensor(ret_rstd[:, :], ret_var[:, :], half_pow[:, :], ALU.pow).then_inc(ret_rstd_ready, 1)
                for m in range(17):
                    n = 0 if m == 0 else (2 if m < 9 else 1)
                    hold_here(pool, inv_ready, l * 17 + m + 1)
                    x = logit[:, m % 4, 0:KEYS[n]]
                    pool.tensor_scalar(x, x, row_inv[:, m:m + 1], None, ALU.mult).then_inc(prob_ready, 1)
                layer_norm(l, 0)
                hold_here(pool, ln_ready, l * 6 + 3)
                load_ln(l, "ln2_g", "ln2_b")
                pool.memset(mo["score"], 0.5).then_inc(moe_clear, 1)
                step(pool.memset(mo["route"], -1.0))
                pool.memset(y_sb[:, 1, :], 0.0).then_inc(moe_clear, 1)
                pool.memset(xg[:, :, :], 0.0).then_inc(moe_clear, 1)
                after_steps()
                pool.tensor_copy(route[:, :, :, 0], k["code"].unsqueeze(2).to_broadcast([128, 3, E_PAD])).then_inc(moe_coded, 1)
                pool.wait_ge(moe_clear, l * 3 + 3)
                pool.wait_ge(h_stored, l * 32 + 32)
                round_(l, 0, False)
                hold_here(pool, count_ready, l + 1)
                most = pool.value_load(count_i[0:1, 0:1], min_val=0, max_val=T)
                with pool.If(most > CAP):
                    with pool.Fori(1, ROUNDS) as r:
                        round_(l, r, True)
                layer_norm(l, 1)
                pool.wait_ge(ln_ready, l * 6 + 6)


_INS = ["x", "meta_tokens", "w_in", "w_uk", "w_uv", "kv_norm_w", "ret_norm_w", "w_o", "ln1_g", "ln1_b", "w_router",
        "router_bias", "w_gate", "w_up", "w_down", "ws_gate", "ws_up", "ws_down", "ln2_g", "ln2_b"]
_OUTS = [((1, SEQ, D), "float32")]


def kernel(**inputs):
    import numpy as _np
    import concourse.bacc as _bacc
    from concourse import mybir as _mybir
    from concourse.bass_utils import run_bass_kernel_spmd as _run

    nc = _bacc.Bacc("TRN2", target_bir_lowering=False, num_devices=1)
    arrays, aps = {}, {}
    for name in _INS + ["consts"]:
        arr = shape_constants() if name == "consts" else _np.ascontiguousarray(inputs[name])
        arrays[f"in_{name}_dram"] = arr
        aps[name] = nc.dram_tensor(f"in_{name}_dram", arr.shape, _mybir.dt.from_np(arr.dtype), kind="ExternalInput").ap()
    shape, dtype = _OUTS[0]
    out = nc.dram_tensor("out_0_dram", shape, _mybir.dt.from_np(_np.dtype(dtype)), kind="ExternalOutput").ap()
    decoder_kernel(nc, aps, out)
    r = _run(nc, [arrays], core_ids=[0])
    return r.results[0]["out_0_dram"]
```

```python
from contextlib import ExitStack

import numpy as np

import concourse.bass as bass
from concourse import mybir

F32 = mybir.dt.float32
I32 = mybir.dt.int32
ALU = mybir.AluOpType
ACT = mybir.ActivationFunctionType
AX = mybir.AxisListType.X

D = 1024
SEQ = 256
DEPTH = 2
META = 16
T = META + SEQ
A_HEADS, A_DIM, LAT = 8, 64, 128
I_HEADS = 8
N_SEL = min(256, SEQ // 4)
R_HEADS, R_QK, R_V = 4, 64, 128
E, GROUPS, TOP_GROUPS = 64, 8, 4
F = 256
EPS = 1e-6
ALPHA = (2 * DEPTH) ** 0.25
ROUTE_SCALE = 2.5
D_IN = 2760
KC = D // 128

CHUNKS = [(0, 16), (16, 128), (144, 128)]
KEYS = [16, 144, 272]
CAP = 64
EXTRA = 4
ROUNDS = 1 + EXTRA
PAIRS = E // 2
E_PAD = E + 4
FAR = 4096.0
NEG = -1e30
TAKEN = -3e38

BLOCKS = [(128 * b, 128) for b in range(9)] + [(1152, 72)] + [(1224 + 128 * b, 128) for b in range(12)]
DOUBLES = [(0, 512, range(0, 4)), (512, 1024, range(4, 8)), (1024, 1480, range(8, 12)),
           (1480, 1992, range(12, 16)), (1992, 2504, range(16, 20)), (2504, 2760, range(20, 22))]
DOUBLE_SLOT = [3, 4, 5, 0, 1, 2]
TURN_BANKS = [(6,), (2, 3), (4, 5)]
OUT_BANKS = [(7,), (2, 3), (0, 1)]
STAGES = 6
SLOT_LOADS = [n + PAIRS // 2 * ROUNDS for n in (1, 1, 1, 2, 2, 1)]

CONSTS = [("ident", 128), ("before", 128), ("ones", 128), ("cos", 96), ("sin", 96), ("decay", 4 * T),
          ("causal", 144 + 272), ("causal0", 16), ("iota", CAP), ("code", 3), ("iota_t", T), ("tri", 64)]
N_CONST = sum(n for _, n in CONSTS)


def shape_constants():
    p = np.arange(128)
    c = {"ident": np.eye(128), "before": p[:, None] < p[None, :], "ones": np.ones((128, 128))}
    half = R_QK // 2
    inv = (np.float32(10000.0) ** (-np.arange(half, dtype=np.float32) / np.float32(half))).astype(np.float32)
    cos, sin = np.zeros((128, 3, half)), np.zeros((128, 3, half))
    for n, (t0, w) in enumerate(CHUNKS):
        ang = ((t0 + p).astype(np.float32)[:, None] * inv).astype(np.float32).astype(np.float64)
        cos[:, n], sin[:, n] = np.cos(ang), np.sin(ang)
    c["cos"], c["sin"] = cos.reshape(128, -1), sin.reshape(128, -1)
    log_g = np.log1p(-np.exp(np.linspace(np.log(1.0 / 32), np.log(1.0 / 512), R_HEADS)))
    ahead = np.arange(T)[None, :] - p[:, None]
    c["decay"] = np.concatenate([np.where(ahead >= 0, np.exp(np.maximum(ahead, 0) * g) * R_QK ** -0.5, 0.0)
                                 for g in log_g], axis=1)
    c["causal"] = np.concatenate([np.where(np.arange(KEYS[n])[None, :] <= CHUNKS[n][0] + p[:, None], 0.0, NEG)
                                  for n in (1, 2)], axis=1)
    c["causal0"] = np.where(np.arange(16)[None, :] <= (p % 16)[:, None], 0.0, NEG)
    c["iota"] = np.tile(np.arange(CAP), (128, 1))
    c["code"] = np.stack([t0 + p - FAR for t0, _ in CHUNKS], axis=1)
    c["iota_t"] = np.tile(np.arange(T) - FAR, (128, 1))
    c["tri"] = np.tile((np.arange(8)[None, :] < np.arange(8)[:, None]).reshape(1, 64), (128, 1))
    return np.concatenate([np.asarray(c[n], np.float64) for n, _ in CONSTS], axis=1).astype(np.float32)


def proj_bank(b):
    return b % 4 if b < 14 else b % 2


def acc_segments(d):
    out, at, end = [], d * T, (d + 1) * T
    while at < end:
        n = min(end, (at // 512 + 1) * 512) - at
        out.append((at // 512, at % 512, at - d * T, n))
        at += n
    return out


def decoder_kernel(nc, a, out):
    ctx = ExitStack()
    with ctx:
        def sb(name, shape, dt=F32):
            return ctx.enter_context(nc.sbuf_tensor(name, shape, dt))

        def sem(name):
            return ctx.enter_context(nc.semaphore(name))

        bank = [ctx.enter_context(nc.psum_tensor(f"bank{i}", [128, 512], F32)) for i in range(8)]

        ring = sb("ring", [128, 6, 4096])
        const = sb("const", [128, N_CONST])
        h_tok = sb("h_tok", [128, 3, D])
        hT = sb("hT", [128, KC, T])
        ln_par = sb("ln_par", [128, 2, D])
        wuk = sb("wuk", [128, 4, LAT])
        wuv = sb("wuv", [128, 8, 64])
        wr = sb("wr", [128, KC * E])
        kvn_w = sb("kvn_w", [128, LAT])
        retn_w = sb("retn_w", [128, R_HEADS * R_V])
        rbias = sb("rbias", [128, E])
        half_pow = sb("half_pow", [128, 12])
        ssq = sb("ssq", [128, 3])
        ckv_var = sb("ckv_var", [128, 3])
        ckv_rstd = sb("ckv_rstd", [128, 3])
        ret_stats = sb("ret_stats", [128, 12, 6])
        ret_mv = sb("ret_mv", [128, 12, 2])
        ret_var = sb("ret_var", [128, 12])
        ret_rstd = sb("ret_rstd", [128, 12])
        ln_sum = sb("ln_sum", [128, 3, 4])
        ln_neg_mean = sb("ln_neg_mean", [128, 3])
        ln_sq = sb("ln_sq", [128, 3])
        ln_var = sb("ln_var", [128, 3])
        ln_rstd = sb("ln_rstd", [128, 3])
        row_max = sb("row_max", [128, 17])
        neg_max = sb("neg_max", [128, 17])
        row_sum = sb("row_sum", [128, 17])
        row_inv = sb("row_inv", [128, 17])
        best8 = sb("best8", [128, 8])

        REGION = 15232
        region = sb("region", [128, REGION])

        def carve(sizes):
            at, views = 0, {}
            for name, n in sizes:
                views[name] = region[:, at:at + n]
                at += n
            assert at <= REGION, at
            return views

        mx = carve([("qa", 4 * T), ("qi", 4 * T), ("kw", T), ("kd", T), ("stage", STAGES * T), ("ckv", 3 * 128),
                    ("ckvT", T), ("wi", 24), ("rot", 3 * 512), ("tmp", 4 * T), ("v", 3 * 512), ("gate", 3 * 512),
                    ("rl", 2 * T), ("qk", 4 * T), ("lat", 8 * T), ("mask", 416), ("work", T)])
        qaT = mx["qa"].rearrange("p (b t) -> p b t", t=T)
        qiT = mx["qi"].rearrange("p (b t) -> p b t", t=T)
        kwT, kdT = mx["kw"], mx["kd"]
        stage = mx["stage"].rearrange("p (b t) -> p b t", t=T)
        ckv = mx["ckv"].rearrange("p (c f) -> p c f", c=3)
        ckvT = mx["ckvT"]
        wi = mx["wi"].rearrange("p (c h) -> p c h", c=3)
        rot = mx["rot"].rearrange("p (c f) -> p c f", c=3)
        rot_a, rot_b = mx["v"][:, 0:512], mx["v"][:, 512:1024]
        v_tok = mx["v"].rearrange("p (c f) -> p c f", c=3)
        gate = mx["gate"].rearrange("p (c f) -> p c f", c=3)
        rl = mx["rl"].rearrange("p (b t) -> p b t", t=T)
        sg_tmp = mx["rl"][:, 0:512]
        qkT = mx["qk"].rearrange("p (b t) -> p b t", t=T)

        def staged(b):
            return qkT[:, b - 18, :] if b >= 18 else stage[:, b % STAGES, :]

        latT = mx["lat"].rearrange("p (h t) -> p h t", t=T)
        masks = {1: mx["mask"][:, 0:144], 2: mx["mask"][:, 144:416]}
        work = mx["work"]
        ln_scratch = region[:, 7656:10728].rearrange("p (b n) -> p b n", b=3)
        mixT = [qaT[:, b, :] for b in range(4)] + [qkT[:, b, :] for b in range(4)]
        decayed = mx["stage"][:, 0:1312].rearrange("p (b n) -> p b n", b=2)
        logit = mx["tmp"].rearrange("p (b t) -> p b t", t=T)
        pT = region[:, 4 * T:4 * T + 4 * 384].rearrange("p (b j q) -> p b j q", b=4, j=3)
        o_ret = rot

        mo = carve([("xg", 2 * D), ("xgT", 2 * 1024), ("y", 2 * 1024), ("selg", 2 * T), ("sel", 384), ("pb", 18), ("idg", 4),
                    ("route", 3 * E_PAD * 3), ("score", 192), ("biased", 192), ("best2", 192), ("grp", 24),
                    ("gt", 192), ("eq", 192), ("rank", 24), ("picked", 192), ("chosen", 192), ("tmp", 192),
                    ("gsum", 3), ("ginv", 3), ("cmax", 1), ("sg", 256), ("ha", 256), ("h", 256), ("h2", 256),
                    ("sgs", 2 * T), ("hs", 2 * T), ("hsT", 2 * T)])
        xg = mo["xg"].rearrange("p (b n) -> p b n", b=2)
        xgT = mo["xgT"].rearrange("p (b k s) -> p b k s", b=2, k=KC)
        y_sb = mo["y"].rearrange("p (b n) -> p b n", b=2)
        selg = mo["selg"].rearrange("p (b t) -> p b t", b=2)
        sel = mo["sel"].rearrange("p (c e s) -> p c e s", c=3, e=2)
        pb = mo["pb"].rearrange("p (c e v) -> p c e v", c=3, e=2)
        idg = mo["idg"].rearrange("p (b v) -> p b v", b=2)
        route = mo["route"].rearrange("p (c e v) -> p c e v", c=3, v=3)
        route_pairs = mo["route"].rearrange("p (c n) -> p c n", c=3)
        rows3 = {n: mo[n].rearrange("p (c e) -> p c e", c=3)
                 for n in ("score", "biased", "best2", "grp", "rank", "picked", "chosen", "tmp")}
        cube = {n: mo[n].rearrange("p (c g e) -> p c g e", c=3, g=8) for n in ("best2", "gt", "eq", "biased")}
        sgs = mo["sgs"].rearrange("p (j t) -> p j t", j=2)
        hs = mo["hs"].rearrange("p (j t) -> p j t", j=2)
        hsT = mo["hsT"].rearrange("p (j t) -> p j t", j=2)
        accT = mx["lat"]
        wsd = mx["lat"][:, 0:2048].rearrange("p (j n) -> p j n", j=2)
        assert sum(v.shape[1] for v in mo.values()) <= 12360
        wsg, wsu = mo["xgT"], mo["y"]
        rank_i = sb("rank_i", [128, 2], I32)
        count_i = sb("count_i", [1, 1], I32)

        k, at = {}, 0
        for name, n in CONSTS:
            k[name] = const[:, at:at + n]
            at += n
        decay = k["decay"].rearrange("p (h t) -> p h t", h=4)
        causal = {1: k["causal"][:, 0:144], 2: k["causal"][:, 144:416]}
        cos3 = k["cos"].rearrange("p (c f) -> p c f", c=3)
        sin3 = k["sin"].rearrange("p (c f) -> p c f", c=3)

        h_rows = nc.dram_tensor("h_rows", [T, D], F32, kind="Internal").ap()

        ident_in = sem("ident_in")
        const_in = sem("const_in")
        h_in = sem("h_in")
        slot_in = [sem(f"slot_in{s}") for s in range(6)]
        small_mix = sem("small_mix")
        small_moe = sem("small_moe")
        ws_down_in = sem("ws_down_in")
        ws_gate_up_in = sem("ws_gate_up_in")
        ln_par_in = sem("ln_par_in")
        proj_done = sem("proj_done")
        proj_act = sem("proj_act")
        proj_dve = sem("proj_dve")
        lat_done = sem("lat_done")
        lat_act = sem("lat_act")
        lat_dve = sem("lat_dve")
        ckv_turned = sem("ckv_turned")
        ckv_ssq = sem("ckv_ssq")
        ckv_var_ready = sem("ckv_var_ready")
        ckv_rstd_ready = sem("ckv_rstd_ready")
        ckv_ready = sem("ckv_ready")
        ckvT_done = sem("ckvT_done")
        ckvT_ready = sem("ckvT_ready")
        wi_turned = sem("wi_turned")
        wi_ready = sem("wi_ready")
        q0_ready = sem("q0_ready")
        index_done = sem("index_done")
        index_relu = sem("index_relu")
        index_added = sem("index_added")
        tok_turned = sem("tok_turned")
        tok_copied = sem("tok_copied")
        gate_sig = sem("gate_sig")
        rot_ready = sem("rot_ready")
        gate_mul = sem("gate_mul")
        gate_ready = sem("gate_ready")
        ret_scores = sem("ret_scores")
        ret_decayed = sem("ret_decayed")
        ret_out = sem("ret_out")
        ret_var_ready = sem("ret_var_ready")
        ret_rstd_ready = sem("ret_rstd_ready")
        ret_ready = sem("ret_ready")
        ret_turned = sem("ret_turned")
        ret_mix = sem("ret_mix")
        logits_done = sem("logits_done")
        logits_masked = sem("logits_masked")
        max_ready = sem("max_ready")
        exp_done = sem("exp_done")
        inv_ready = sem("inv_ready")
        prob_ready = sem("prob_ready")
        prob_turned = sem("prob_turned")
        prob_copied = sem("prob_copied")
        olat_done = sem("olat_done")
        olat_ready = sem("olat_ready")
        out_a_done = sem("out_a_done")
        w_o_half_used = sem("w_o_half_used")
        out_a_ready = sem("out_a_ready")
        sub_done = sem("sub_done")
        ln_mean_ready = sem("ln_mean_ready")
        ln_sq_ready = sem("ln_sq_ready")
        ln_rstd_ready = sem("ln_rstd_ready")
        ln_ready0 = sem("ln_ready0")
        ln_ready = sem("ln_ready")
        hT_turned = sem("hT_turned")
        hT_act = sem("hT_act")
        hT_dve = sem("hT_dve")
        h_stored = sem("h_stored")
        moe_clear = sem("moe_clear")
        y_clear = sem("y_clear")
        moe_coded = sem("moe_coded")
        router_done = sem("router_done")
        score_ready = sem("score_ready")
        chosen_ready = sem("chosen_ready")
        gates_ready = sem("gates_ready")
        rank_done = sem("rank_done")
        rank_ready = sem("rank_ready")
        count_ready = sem("count_ready")
        shared_done = sem("shared_done")
        shared_sig = sem("shared_sig")
        shared_ready = sem("shared_ready")
        gates_used = sem("gates_used")
        gu_done = sem("gu_done")
        xta_done = sem("xta_done")
        xtb_done = sem("xtb_done")
        ht_done = sem("ht_done")
        y_done = sem("y_done")
        scattered = sem("scattered")
        slot_row_done = sem("slot_row_done")
        sig_ready = sem("sig_ready")
        xta_ready = sem("xta_ready")
        y_ready = sem("y_ready")
        shifted = sem("shifted")
        selg_ready = sem("selg_ready")
        pair_ready = sem("pair_ready")
        sel_ready = sem("sel_ready")
        ha_ready = sem("ha_ready")
        h_ready = sem("h_ready")
        xtb_ready = sem("xtb_ready")
        ht_ready = sem("ht_ready")
        idg_ready = sem("idg_ready")
        slot_row_ready = sem("slot_row_ready")
        gathered = [sem(f"gathered{i}") for i in range(2)]
        gather_over = sem("gather_over")
        acc_act = sem("acc_act")
        acc_dve = sem("acc_dve")
        out_stored = sem("out_stored")
        dve_step = sem("dve_step")
        pool_step = sem("pool_step")
        passed = sem("passed")

        def hold_here(eng, s, value):
            eng.wait_ge(s, value)
            eng.sem_inc(passed, 1)

        w_in_v = a["w_in"].rearrange("l (p k) n -> l p k n", k=KC)
        w_o_v = a["w_o"].rearrange("l (k p) n -> l p k n", p=128)
        gate_v = a["w_gate"].rearrange("l (q e) (p k) f -> (l q) p e (k f)", e=2, k=KC)
        up_v = a["w_up"].rearrange("l (q e) (p k) f -> (l q) p e (k f)", e=2, k=KC)
        down_v = a["w_down"].rearrange("l (q e) (j p) n -> (l q) p (e j) n", e=2, p=128)
        wsg_v = a["ws_gate"].rearrange("l (p k) f -> l p (k f)", k=KC)
        wsu_v = a["ws_up"].rearrange("l (p k) f -> l p (k f)", k=KC)
        wsd_v = a["ws_down"].rearrange("l (j p) n -> l p j n", p=128)

        def slot(s, at, n):
            return ring[:, s, at:at + n]

        block = ctx.enter_context(nc.Block())

        @block.sync
        def _(sp):
            sp.dma_start(const[:, 0:128], a["consts"][:, 0:128]).then_inc(ident_in, 16)
            sp.dma_start(h_tok[0:META, 0, :], a["meta_tokens"]).then_inc(h_in, 16)
            sp.dma_start(h_tok[:, 1:3, :], a["x"].rearrange("b (c p) d -> p (b c) d", p=128)).then_inc(h_in, 16)

            def load_pair(l, r, i, u, part, first):
                g = l * ROUNDS + r
                s = part if u == 0 else 3 + part
                if not first:
                    used, per = ((gates_used, 1), (gu_done, 1), (y_done, 2))[part]
                    sp.wait_ge(used, per * (g * PAIRS + i * 2 + u - 1))
                q = l * PAIRS + i * 2 + u
                src = (gate_v, up_v, down_v)[part][bass.ds(q, 1)]
                if part < 2:
                    src = src.rearrange("o p e n -> (o p) e n")
                    dst = ring[:, s, :].rearrange("p (e n) -> p e n", e=2)
                else:
                    src = src.rearrange("o p e n -> (o p) e n")
                    dst = ring[:, s, :].rearrange("p (e n) -> p e n", e=4)
                sp.dma_start(dst, src).then_inc(slot_in[s], 16)

            with sp.Fori(0, DEPTH) as l:
                for n, (c0, c1, _) in enumerate(DOUBLES):
                    if n == 0:
                        sp.wait_ge(y_done, l * (2 * PAIRS * ROUNDS))
                    if n == 2:
                        sp.wait_ge(small_mix, l * 64 + 64)
                    s, w = DOUBLE_SLOT[n], c1 - c0
                    src = w_in_v[bass.ds(l, 1), :, :, c0:c1].rearrange("l p k n -> (l p) k n")
                    sp.dma_start(slot(s, 0, KC * w).rearrange("p (k n) -> p k n", k=KC), src).then_inc(slot_in[s], 16)
                for n in range(2):
                    sp.wait_ge(proj_done, l * 22 + 4 * (n + 1))
                    src = w_o_v[bass.ds(l, 1), :, 4 * n:4 * n + 4, :].rearrange("l p k n -> (l p) k n")
                    sp.dma_start(ring[:, 3 + n, :].rearrange("p (k n) -> p k n", k=4), src).then_inc(slot_in[3 + n], 16)
                sp.wait_ge(proj_done, l * 22 + 12)
                load_pair(l, 0, 0, 1, 2, True)
                sp.wait_ge(proj_done, l * 22 + 16)
                load_pair(l, 0, 0, 0, 0, True)
                sp.wait_ge(proj_done, l * 22 + 20)
                load_pair(l, 0, 0, 0, 1, True)
                sp.wait_ge(proj_done, l * 22 + 22)
                load_pair(l, 0, 0, 0, 2, True)
                sp.wait_ge(out_a_done, l * 4 + 4)
                sp.dma_start(wsd, wsd_v[bass.ds(l, 1)].rearrange("l p j n -> (l p) j n")).then_inc(ws_down_in, 16)
                sp.wait_ge(ret_turned, l * 3 + 3)
                sp.dma_start(wsg, wsg_v[bass.ds(l, 1)].rearrange("l p n -> (l p) n")).then_inc(ws_gate_up_in, 16)
                sp.dma_start(wsu, wsu_v[bass.ds(l, 1)].rearrange("l p n -> (l p) n")).then_inc(ws_gate_up_in, 16)
                sp.wait_ge(w_o_half_used, l + 1)
                load_pair(l, 0, 0, 1, 0, True)
                sp.wait_ge(sub_done, l * 6 + 3)
                load_pair(l, 0, 0, 1, 1, True)
                with sp.Fori(1, PAIRS // 2) as i:
                    for u in range(2):
                        for part in range(3):
                            load_pair(l, 0, i, u, part, False)
                hold_here(sp, count_ready, l + 1)
                most = sp.value_load(count_i[0:1, 0:1], min_val=0, max_val=T)
                with sp.If(most > CAP):
                    with sp.Fori(1, ROUNDS) as r:
                        with sp.Fori(0, PAIRS // 2) as i:
                            for u in range(2):
                                for part in range(3):
                                    load_pair(l, r, i, u, part, False)
                with sp.Else():
                    for s in range(6):
                        sp.wait_ge(slot_in[s], l * (16 * SLOT_LOADS[s]) + 16 * (SLOT_LOADS[s] - 16 * EXTRA))
                        sp.sem_inc(slot_in[s], 16 * 16 * EXTRA)
            sp.wait_ge(ln_ready, DEPTH * 4)
            sp.dma_start(out.rearrange("b (c p) d -> p (b c) d", p=128), h_tok[:, 1:3, :]).then_inc(out_stored, 16)
            sp.wait_ge(out_stored, 16)

        @block.tensor
        def _(pe):
            ident = k["ident"]
            mm = pe.matmul

            def turn_h(l=None, ph=0):
                for n, (t0, w) in enumerate(CHUNKS):
                    if l is not None:
                        hold_here(pe, ln_ready if n else ln_ready0, l * 4 + ph * 2 + n if n else l * 2 + ph + 1)
                    rows = h_tok[0:w, n, :].rearrange("t (p k) -> t k p", k=KC)
                    for half in range(1 if n == 0 else 2):
                        per = KC if n == 0 else 4
                        for j in range(per):
                            last = pe.transpose(bank[TURN_BANKS[n][half]][:, j * w:(j + 1) * w], rows[:, half * 4 + j, :],
                                                ident[0:w, 0:w])
                        last.then_inc(hT_turned, 1)

            rounds_run = pe.alloc_register("rounds_run")
            pe.reg_mov(rounds_run, 0)

            pe.wait_ge(ident_in, 16)
            pe.wait_ge(h_in, 32)
            turn_h()

            def slot_rows(g, q, before, evac):
                pe.wait_ge(before, evac)
                pe.wait_ge(sel_ready, g * 34 + q + 1)
                for e in range(2):
                    for n, (t0, w) in enumerate(CHUNKS):
                        last = mm(bank[7][64 * e:64 * e + 64, 0:2], sel[0:w, n, e, :], pb[0:w, n, e, 0:2],
                                  start=(n == 0), stop=(n == 2))
                last.then_inc(slot_row_done, 1)

            def round_(l, r, extra):
                g = l * ROUNDS + r
                past = pe.snap(rounds_run)

                def turn_x(q, u, part, before, evac):
                    pe.wait_ge(before, evac)
                    rows = xg[:, u, :].rearrange("s (p k) -> s k p", k=KC)
                    for j in range(4):
                        last = pe.transpose(bank[7][:, j * 128:(j + 1) * 128], rows[:, 4 * part + j, :], ident)
                    last.then_inc((xta_done, xtb_done)[part], 1)

                opened = set()

                def scatter(u, ds, last_of_pair, stop=False, opens=False):
                    for d in ds:
                        for b, c, t, n in acc_segments(d):
                            last = mm(bank[b][:, c:c + n], y_sb[:, u, d * 128:(d + 1) * 128], selg[:, u, t:t + n],
                                      start=opens and b not in opened, stop=stop, skip_group_check=True)
                            opened.add(b)
                    if last_of_pair:
                        last.then_inc(scattered, 1)

                if extra:
                    slot_rows(g, 0, ht_ready, g * 32)
                    slot_rows(g, 1, slot_row_ready, g * 34 + 1)
                pe.wait_ge(gathered[0], past * (16 * 17) + 16)
                turn_x(0, 0, 0, slot_row_ready, g * 34 + 2)
                turn_x(0, 0, 1, xta_ready, g * 33 + 1)

                def two_pairs(i, first):
                    for u in range(2):
                        opens = first and u == 0
                        p = i * 2 + u
                        base = 0 if u == 0 else 3
                        before = [SLOT_LOADS[base + j] - 16 * ROUNDS for j in range(3)]
                        arrived = [l * (16 * SLOT_LOADS[base + j]) + r * 256 + i * 16
                                   + 16 * (before[j] + 1) for j in range(3)]
                        pe.wait_ge(slot_in[base], arrived[0])
                        pe.wait_ge(xtb_ready, g * 33 + p + 1)
                        pe.wait_ge(xta_ready, g * 33 + p + 1)
                        pe.wait_ge(h_ready, g * 32 + p)
                        for part in range(2):
                            if part == 1:
                                slot_rows(g, p + 2, ht_ready, g * 32 + p)
                                pe.wait_ge(slot_in[base + 1], arrived[1])
                            w = ring[:, base + part, :].rearrange("p (e k f) -> p e k f", e=2, k=KC)
                            for kk in range(KC):
                                for e in range(2):
                                    last = mm(bank[5][64 * e:64 * e + 64, part * F:(part + 1) * F],
                                              xgT[:, u, kk, 64 * e:64 * e + 64], w[:, e, kk, :],
                                              start=(kk == 0), stop=(kk == KC - 1))
                            last.then_inc((gates_used, gu_done)[part], 1)
                        pe.wait_ge(gathered[1 - u], past * (16 * 17) + ((i + u) * 16 + 16))
                        turn_x(p + 1, 1 - u, 0, slot_row_ready, g * 34 + p + 3)
                        if opens:
                            pe.wait_ge(y_clear, l + 1)
                            pe.wait_ge(shared_ready, l * 2 + 2)
                        pe.wait_ge(y_ready, g * 64 + p * 2)
                        pe.wait_ge(selg_ready, g * 33 + p + 1)
                        scatter(1 - u, range(0, 4), False, opens=opens)
                        turn_x(p + 1, 1 - u, 1, xta_ready, g * 33 + p + 2)
                        pe.wait_ge(h_ready, g * 32 + p + 1)
                        pe.wait_ge(xtb_ready, g * 33 + p + 2)
                        for j in range(2):
                            last = pe.transpose(bank[7][:, j * 128:(j + 1) * 128], mo["h"][:, j * 128:(j + 1) * 128], ident)
                        last.then_inc(ht_done, 1)
                        scatter(1 - u, range(4, 6), False, opens=opens)
                        pe.wait_ge(ht_ready, g * 32 + p + 1)
                        pe.wait_ge(slot_in[base + 2], arrived[2])
                        w = ring[:, base + 2, :].rearrange("p (e j n) -> p e j n", e=2, j=2)
                        for half in range(2):
                            pe.wait_ge(y_ready, g * 64 + p * 2 + half)
                            for j in range(2):
                                for e in range(2):
                                    last = mm(bank[6][64 * e:64 * e + 64, :],
                                              mo["h2"][:, j * 128 + 64 * e:j * 128 + 64 * e + 64],
                                              w[:, e, j, half * 512:(half + 1) * 512], start=(j == 0), stop=(j == 1))
                            last.then_inc(y_done, 1)
                            if half == 0:
                                scatter(1 - u, range(6, 8), True, opens=opens)
                if extra:
                    with pe.Fori(0, PAIRS // 2) as i:
                        two_pairs(i, False)
                else:
                    two_pairs(0, True)
                    with pe.Fori(1, PAIRS // 4) as i:
                        two_pairs(i, False)
                    pe.wait_ge(ws_down_in, l * 16 + 16)
                    for d in range(8):
                        for b, c, t, n in acc_segments(d):
                            for j in range(2):
                                mm(bank[b][:, c:c + n], wsd[:, j, d * 128:(d + 1) * 128], hsT[:, j, t:t + n],
                                   start=False, stop=False, skip_group_check=True)
                    with pe.Fori(PAIRS // 4, PAIRS // 2) as i:
                        two_pairs(i, False)
                pe.wait_ge(y_ready, g * 64 + 64)
                pe.wait_ge(selg_ready, g * 33 + 33)
                scatter(1, range(0, 8), True, stop=True)
                pe.reg_add(rounds_run, rounds_run, 1)

            with pe.Fori(0, DEPTH) as l:
                pe.wait_ge(hT_act, l * 6 + 3)
                pe.wait_ge(hT_dve, l * 4 + 2)

                def evacuated(b):
                    if b >= 10 or b % 2 == 0:
                        pe.wait_ge(proj_act, l * 17 + (b // 2 + 1 if b < 10 else b - 4))
                    else:
                        pe.wait_ge(proj_dve, l * 5 + b // 2 + 1)

                def project(b):
                    n = next(i for i, dd in enumerate(DOUBLES) if b in dd[2])
                    c0, c1, blocks = DOUBLES[n]
                    s = DOUBLE_SLOT[n]
                    if b == blocks[0]:
                        pe.wait_ge(slot_in[s], l * (16 * SLOT_LOADS[s]) + 16)
                    if b >= 4:
                        evacuated(b - (4 if b < 14 else 2))
                    w = slot(s, 0, KC * (c1 - c0)).rearrange("p (k n) -> p k n", k=KC)
                    at, width = BLOCKS[b][0] - c0, BLOCKS[b][1]
                    for kk in range(KC):
                        last = mm(bank[proj_bank(b)][0:width, 0:T], w[:, kk, at:at + width], hT[:, kk, :],
                                  start=(kk == 0), stop=(kk == KC - 1))
                    last.then_inc(proj_done, 1)

                for b in range(5):
                    project(b)
                pe.wait_ge(small_mix, l * 64 + 64)
                for h in range(A_HEADS):
                    if h % 2 == 0:
                        evacuated(h // 2)
                    if h >= 4:
                        pe.wait_ge((lat_act, lat_dve)[h % 2], l * 4 + (h - 4) // 2 + 1)
                    r = 64 * (h % 2)
                    mm(bank[4 + h % 4][:, 0:T], wuk[r:r + 64, h // 2, :], qaT[r:r + 64, h // 2, :],
                       start=True, stop=True).then_inc(lat_done, 1)
                for b in range(5, 8):
                    project(b)
                pe.wait_ge(proj_act, l * 17 + 3)
                pe.wait_ge(lat_act, l * 4 + 3)
                for n, (t0, w) in enumerate(CHUNKS):
                    last = pe.transpose(bank[4][0:w, n * 128:(n + 1) * 128], stage[:, 4 % STAGES, t0:t0 + w], ident)
                last.then_inc(ckv_turned, 1)
                for b in range(8, 10):
                    project(b)
                evacuated(9)
                pe.wait_ge(lat_dve, l * 4 + 3)
                for n in (1, 2):
                    t0, w = CHUNKS[n]
                    last = pe.transpose(bank[5][0:w, n * 72:(n + 1) * 72], kwT[0:72, t0:t0 + w], ident[0:72, 0:72])
                last.then_inc(wi_turned, 1)
                pe.wait_ge(ckv_ready, l * 3 + 3)
                hold_here(pe, lat_act, l * 4 + 4)
                for n, (t0, w) in enumerate(CHUNKS):
                    last = pe.transpose(bank[6][:, t0:t0 + w], ckv[0:w, n, :], ident[0:w, 0:w])
                last.then_inc(ckvT_done, 1)

                def index_scores(n, first):
                    t0, w = CHUNKS[n]
                    for h in range(I_HEADS):
                        m = first + h
                        if m == 0:
                            pe.wait_ge(wi_ready, l + 1)
                            pe.wait_ge(ckvT_ready, l + 1)
                            pe.wait_ge(lat_dve, l * 4 + 4)
                            evacuated(5)
                            evacuated(7)
                            evacuated(8)
                        if m >= 4:
                            pe.wait_ge(index_relu, l * 16 + m - 3)
                        r = 64 * (h % 2)
                        keys = kdT if h % 2 else kwT
                        mm(bank[4 + m % 4][:, 0:KEYS[n]], qiT[r:r + 64, h // 2, t0:t0 + w], keys[r:r + 64, 0:KEYS[n]],
                           start=True, stop=True).then_inc(index_done, 1)

                index_scores(2, 0)
                for b in (10, 11, 12):
                    project(b)
                index_scores(1, 8)
                project(13)

                def turn_group(j0, b0):
                    evacuated(b0 + 3)
                    for n, (t0, w) in enumerate(CHUNKS):
                        j = j0 + n
                        if j == 0:
                            pe.wait_ge(index_relu, l * 16 + 16)
                        if j == 3:
                            pe.wait_ge(prob_copied, l * 17 + 17)
                            pe.wait_ge(olat_ready, l * 5 + 5)
                        if j >= 4:
                            pe.wait_ge(tok_copied, l * 12 + j - 3)
                        for c in range(4):
                            last = pe.transpose(bank[4 + j % 4][0:w, c * 128:(c + 1) * 128],
                                                staged(b0 + c)[:, t0:t0 + w], ident)
                        last.then_inc(tok_turned, 1)

                turn_group(0, 10)
                project(14)

                jobs = [(0, None)] + [(2, h) for h in range(8)] + [(1, h) for h in range(8)]

                def logits(m):
                    n, h = jobs[m]
                    if m >= 2:
                        pe.wait_ge(logits_masked, l * 17 + m - 1)
                    elif m == 0:
                        evacuated(11)
                    t0, w = CHUNKS[n]
                    if m == 0:
                        pe.wait_ge(q0_ready, l + 1)
                    q = work[:, 0:128] if n == 0 else latT[:, h, t0:t0 + w]
                    mm(bank[2 + m % 2][:, 0:KEYS[n]], q, ckvT[:, 0:KEYS[n]], start=True, stop=True).then_inc(logits_done, 1)

                def turn_probs(m):
                    n, _ = jobs[m]
                    pe.wait_ge(prob_ready, l * 17 + m + 1)
                    if m >= 2:
                        pe.wait_ge(prob_copied, l * 17 + m - 1)
                    elif m == 0:
                        pe.wait_ge(tok_copied, l * 12 + 3)
                    for j in range(n + 1):
                        t0, w = CHUNKS[j]
                        last = pe.transpose(bank[4 + m % 2][0:w, j * 128:(j + 1) * 128], logit[:, m % 4, t0:t0 + w], ident)
                    last.then_inc(prob_turned, 1)

                def out_latent(m):
                    n, h = jobs[m]
                    pe.wait_ge(prob_copied, l * 17 + m + 1)
                    group = (m + 3) // 4
                    if group >= 2 and (m - 1) % 4 == 0:
                        pe.wait_ge(olat_ready, l * 5 + group - 1)
                    c = 0 if m == 0 else (m - 1) % 4 * 128
                    for j in range(n + 1):
                        w = CHUNKS[j][1]
                        last = mm(bank[7 - group % 2][:, c:c + 128], ckv[0:w, j, :], pT[0:w, m % 4, j, :],
                                  start=(j == 0), stop=(j == n))
                    last.then_inc(olat_done, 1)

                for m in range(17 + 4):
                    if m < 17:
                        logits(m)
                    if 0 <= m - 3 < 17:
                        turn_probs(m - 3)
                    if m >= 4:
                        out_latent(m - 4)
                    if m % 2 == 0 and 2 <= m <= 14:
                        project(14 + m // 2)

                turn_group(3, 14)
                turn_group(6, 18)
                for n, (t0, w) in enumerate(CHUNKS):
                    j = 9 + n
                    pe.wait_ge(tok_copied, l * 12 + j - 3)
                    hold_here(pe, rot_ready, l * 3 + n + 1)
                    for c in range(4):
                        last = pe.transpose(bank[4 + j % 4][:, c * w:(c + 1) * w], rot[0:w, n, c * 128:(c + 1) * 128],
                                            ident[0:w, 0:w])
                    last.then_inc(tok_turned, 1)

                pe.wait_ge(tok_copied, l * 12 + 12)
                hold_here(pe, proj_act, l * 17 + 17)
                hold_here(pe, logits_masked, l * 17 + 17)

                def ret_score(h):
                    r, c, b = 64 * (h % 2), h // 2, 2 * (h % 2)
                    if h >= 2:
                        hold_here(pe, ret_decayed, l * 12 + 3 * (h - 1))
                    mm(bank[b][0:16, 0:T], qkT[r:r + 64, 2 + c, 0:16], qkT[r:r + 64, c, 0:T],
                       start=True, stop=True).then_inc(ret_scores, 1)
                    mm(bank[b + 1][:, 0:256], qkT[r:r + 64, 2 + c, 16:144], qkT[r:r + 64, c, 16:T], start=True, stop=True)
                    mm(bank[b + 1][:, 256:384], qkT[r:r + 64, 2 + c, 144:T], qkT[r:r + 64, c, 144:T],
                       start=True, stop=True).then_inc(ret_scores, 1)

                def ret_value(h):
                    hold_here(pe, ret_decayed, l * 12 + 3 * (h + 1))
                    dec = decayed[:, h % 2, :]
                    vs = slice(h * 128, (h + 1) * 128)
                    for n, (t0, w) in enumerate(CHUNKS):
                        parts = [(dec[0:16, t0:t0 + w], v_tok[0:16, 0, vs])]
                        if n >= 1:
                            parts.append((dec[:, T + t0 - 16:T + t0 - 16 + w], v_tok[:, 1, vs]))
                        if n == 2:
                            parts.append((dec[:, T + 256:T + 384], v_tok[:, 2, vs]))
                        for m, (s, v) in enumerate(parts):
                            last = mm(bank[4 + n][0:w, vs], s, v, start=(m == 0), stop=(m == n))
                    last.then_inc(ret_out, 1)

                for h in range(R_HEADS):
                    ret_score(h)
                    if h:
                        ret_value(h - 1)
                ret_value(R_HEADS - 1)

                hold_here(pe, ret_decayed, l * 12 + 12)
                for h in range(A_HEADS):
                    r = 64 * (h % 2)
                    last = mm(bank[h // 2][r:r + 64, 0:T], wuv[:, h, :], latT[:, h, :], start=True, stop=True)
                    if h % 2:
                        last.then_inc(out_a_done, 1)

                def project_out(n, kks):
                    t0, w = CHUNKS[n]
                    for half, b in enumerate(OUT_BANKS[n]):
                        for kk in kks:
                            wo = ring[:, 3 + kk // 4, :].rearrange("p (k n) -> p k n", k=4)
                            for q in range(4 if n == 0 else 1):
                                if n == 0:
                                    o, c0, cols = bank[b][32 * q:32 * q + w, 0:256], q * 256, 256
                                else:
                                    o, c0, cols = bank[b][0:w, :], half * 512, 512
                                last = mm(o, mixT[kk][:, t0:t0 + w], wo[:, kk % 4, c0:c0 + cols],
                                          start=(kk == 0), stop=(kk == KC - 1))
                    return last

                pe.wait_ge(out_a_ready, l * 4 + 4)
                pe.wait_ge(slot_in[3], l * (16 * SLOT_LOADS[3]) + 32)
                pe.wait_ge(tok_copied, l * 12 + 12)
                for n in range(2):
                    project_out(n, range(4))
                for n, (t0, w) in enumerate(CHUNKS):
                    hold_here(pe, ret_ready, l * 3 + n + 1)
                    for c in range(4):
                        last = pe.transpose(bank[4 + n][:, c * w:(c + 1) * w], o_ret[0:w, n, c * 128:(c + 1) * 128],
                                            ident[0:w, 0:w])
                    last.then_inc(ret_turned, 1)
                project_out(2, range(4)).then_inc(w_o_half_used, 1)
                pe.wait_ge(ret_mix, l * 3 + 3)
                pe.wait_ge(slot_in[4], l * (16 * SLOT_LOADS[4]) + 32)
                for n in range(3):
                    project_out(n, range(4, KC)).then_inc(sub_done, 1)
                turn_h(l, 0)

                pe.wait_ge(hT_act, l * 6 + 6)
                pe.wait_ge(hT_dve, l * 4 + 4)
                pe.wait_ge(small_moe, l * 32 + 32)
                wr3 = wr[:, :].rearrange("p (k e) -> p k e", k=KC)
                for n, (t0, w) in enumerate(CHUNKS):
                    for kk in range(KC):
                        last = mm(bank[6][0:w, n * E:(n + 1) * E], hT[:, kk, t0:t0 + w], wr3[:, kk, :],
                                  start=(kk == 0), stop=(kk == KC - 1))
                last.then_inc(router_done, 1)
                pe.wait_ge(ws_gate_up_in, l * 32 + 32)
                for j in range(2):
                    if j == 1:
                        pe.wait_ge(const_in, 16)
                        hold_here(pe, chosen_ready, l + 1)
                        ch = rows3["chosen"]
                        for n, (t0, w) in enumerate(CHUNKS):
                            for m in range(n + 1):
                                wm = CHUNKS[m][1]
                                mm(bank[5][0:w, n * E:(n + 1) * E], k["before" if m == n else "ones"][0:wm, 0:w],
                                   ch[0:wm, m, :], start=(m == 0), stop=(m == n))
                        for m in range(3):
                            wm = CHUNKS[m][1]
                            last = mm(bank[5][:, 3 * E:4 * E], k["ones"][0:wm, :], ch[0:wm, m, :],
                                      start=(m == 0), stop=(m == 2))
                        last.then_inc(rank_done, 1)
                    for part in range(2):
                        w = (wsg, wsu)[part].rearrange("p (k f) -> p k f", k=KC)
                        for kk in range(KC):
                            last = mm(bank[2 * j + part][:, 0:T], w[:, kk, j * 128:(j + 1) * 128], hT[:, kk, :],
                                      start=(kk == 0), stop=(kk == KC - 1))
                            if j == 1 and (part, kk) in ((0, KC - 1), (1, 3)):
                                slot_rows(l * ROUNDS, part, slot_row_ready, l * (ROUNDS * 34) + part)
                    last.then_inc(shared_done, 1)
                pe.wait_ge(rank_ready, l + 1)
                pe.wait_ge(score_ready, l * 2 + 2)
                round_(l, 0, False)
                hold_here(pe, count_ready, l + 1)
                most = pe.value_load(count_i[0:1, 0:1], min_val=0, max_val=T)
                with pe.If(most > CAP):
                    with pe.Fori(1, ROUNDS) as r:
                        round_(l, r, True)
                with pe.Else():
                    for s, per in ((gates_used, 32), (gu_done, 32), (xta_done, 33), (xtb_done, 33), (ht_done, 32),
                                   (y_done, 64), (scattered, 33), (slot_row_done, 34)):
                        pe.wait_ge(s, l * (ROUNDS * per) + per)
                        pe.sem_inc(s, EXTRA * per)

                pe.wait_ge(acc_act, l * 3 + 3)
                pe.wait_ge(acc_dve, l * 2 + 2)
                for n, (t0, w) in enumerate(CHUNKS):
                    for d in range(8):
                        last = pe.transpose(bank[2 * n + d // 4][0:w, d % 4 * 128:(d % 4 + 1) * 128],
                                            accT[:, d * T + t0:d * T + t0 + w], ident)
                    last.then_inc(sub_done, 1)
                turn_h(l, 1)

        @block.scalar
        def _(act):
            def copy(o, i, s):
                act.activation(o, i, ACT.Copy).then_inc(s, 1)

            def h_feature(base):
                for j, (n, at) in enumerate(((0, 1), (1, 2), (2, 4))):
                    t0, w = CHUNKS[n]
                    act.wait_ge(hT_turned, base * 5 + at)
                    kk = KC if n == 0 else 4
                    copy(hT[:, 0:kk, t0:t0 + w], bank[TURN_BANKS[n][0]][:, 0:kk * w].rearrange("p (k t) -> p k t", k=kk), hT_act)

            h_feature(0)

            def layer_norm(l, ph):
                base = l * 6 + ph * 3
                for n, (t0, w) in enumerate(CHUNKS):
                    act.wait_ge(ln_mean_ready, base + n + 1)
                    if n:
                        act.wait_ge(ln_sq_ready, base + n)
                    act.activation(ln_scratch[0:w, 0, :], h_tok[0:w, n, :], ACT.Square, bias=ln_neg_mean[0:w, n:n + 1],
                                   accum_out=ln_sq[0:w, n:n + 1]).then_inc(ln_sq_ready, 1)

            def round_(l, r):
                g = l * ROUNDS + r
                def turned(q, u):
                    act.wait_ge(xta_done, g * 33 + q + 1)
                    act.activation(xgT[:, u, 0:4, :], bank[7][:, :].rearrange("p (k s) -> p k s", k=4), ACT.Copy)\
                        .then_inc(xta_ready, 1)

                turned(0, 0)
                with act.Fori(0, PAIRS // 2) as i:
                    for u in range(2):
                        p = i * 2 + u
                        act.wait_ge(ha_ready, g * 32 + p)
                        act.wait_ge(gu_done, g * 32 + p + 1)
                        act.activation(mo["sg"], bank[5][:, 0:F], ACT.Sigmoid).then_inc(sig_ready, 1)
                        turned(p + 1, 1 - u)
                        act.wait_ge(scattered, g * 33 + p)
                        for half in range(2):
                            act.wait_ge(y_done, g * 64 + p * 2 + half + 1)
                            act.activation(y_sb[:, u, half * 512:(half + 1) * 512], bank[6][:, :], ACT.Copy)\
                                .then_inc(y_ready, 1)

            with act.Fori(0, DEPTH) as l:
                def proj(b):
                    act.wait_ge(proj_done, l * 22 + b + 1)
                    if b == 16:
                        act.wait_ge(tok_turned, l * 12 + 3)
                    if b < 4:
                        dst = qaT[:, b, :]
                    elif b in (6, 8):
                        dst = qiT[:, b - 5, :]
                    else:
                        dst = staged(b)
                    copy(dst, bank[proj_bank(b)][:, 0:T], proj_act)

                for b in (0, 2, 4):
                    proj(b)
                for h in (0, 2, 4, 6):
                    act.wait_ge(lat_done, l * 8 + h + 1)
                    copy(latT[:, h, :], bank[4 + h % 4][:, 0:T], lat_act)
                proj(6)
                act.wait_ge(ckv_turned, l + 1)
                for n, (t0, w) in enumerate(CHUNKS):
                    if n:
                        act.wait_ge(ckv_ssq, l * 3 + n)
                    act.activation(rl[0:w, 0, 0:128], bank[4][0:w, n * 128:(n + 1) * 128], ACT.Square,
                                   accum_out=ssq[0:w, n:n + 1]).then_inc(ckv_ssq, 1)
                proj(8)
                act.wait_ge(ckv_ssq, l * 3 + 3)

                def relu(n, first):
                    for h in range(I_HEADS):
                        m = first + h
                        act.wait_ge(index_done, l * 16 + m + 1)
                        if m >= 2:
                            act.wait_ge(index_added, l * 16 + m - 1)
                        act.activation(rl[:, m % 2, 0:KEYS[n]], bank[4 + m % 4][:, 0:KEYS[n]], ACT.Relu)\
                            .then_inc(index_relu, 1)

                relu(2, 0)
                for b in (10, 11, 12):
                    proj(b)
                relu(1, 8)
                proj(13)

                def token_major(j0, dst):
                    for n, (t0, w) in enumerate(CHUNKS):
                        act.wait_ge(tok_turned, l * 12 + j0 + n + 1)
                        copy(dst[0:w, n, :], bank[4 + (j0 + n) % 4][0:w, :], tok_copied)

                token_major(0, rot)
                proj(14)

                def probs(m):
                    n = 0 if m == 0 else (2 if m < 9 else 1)
                    act.wait_ge(prob_turned, l * 17 + m + 1)
                    if m >= 4:
                        act.wait_ge(olat_done, l * 17 + m - 3)
                    b = bank[4 + m % 2]
                    first = act.activation(pT[0:16, m % 4, 0, :], b[0:16, 0:128], ACT.Copy)
                    if n == 0:
                        first.then_inc(prob_copied, 1)
                    else:
                        act.activation(pT[:, m % 4, 1:n + 1, :], b[:, 128:(n + 1) * 128].rearrange("p (j q) -> p j q", j=n),
                                       ACT.Copy).then_inc(prob_copied, 1)

                def job_probs(m):
                    n = 0 if m == 0 else (2 if m < 9 else 1)
                    return logit[:, m % 4, 0:KEYS[n]]

                for m in range(17 + 2):
                    if m < 17:
                        x = job_probs(m)
                        act.wait_ge(max_ready, l * 17 + m + 1)
                        act.activation(x, x, ACT.Exp, bias=neg_max[:, m:m + 1], scale=A_DIM ** -0.5,
                                       accum_out=row_sum[:, m:m + 1]).then_inc(exp_done, 1)
                    if 1 <= m <= 17:
                        x = job_probs(m - 1)
                        act.wait_ge(inv_ready, l * 17 + m)
                        act.activation(x, x, ACT.Copy, scale=row_inv[:, m - 1:m]).then_inc(prob_ready, 1)
                    if m % 2 == 0 and 2 <= m <= 14:
                        proj(14 + m // 2)
                    if m >= 2:
                        probs(m - 2)
                act.wait_ge(rot_ready, l * 3 + 3)
                token_major(3, v_tok)
                token_major(6, gate)
                for n, (t0, w) in enumerate(CHUNKS):
                    j = 9 + n
                    act.wait_ge(tok_turned, l * 12 + j + 1)
                    copy(qkT[:, :, t0:t0 + w], bank[4 + j % 4][:, 0:4 * w].rearrange("p (c t) -> p c t", c=4), tok_copied)
                act.wait_ge(index_added, l * 16 + 16)
                for n, (t0, w) in enumerate(CHUNKS):
                    if n:
                        act.wait_ge(gate_mul, l * 3 + n)
                    act.wait_ge(tok_copied, l * 12 + 9)
                    act.activation(sg_tmp[0:w, :], gate[0:w, n, :], ACT.Sigmoid).then_inc(gate_sig, 1)
                for b in range(4):
                    act.wait_ge(out_a_done, l * 4 + b + 1)
                    copy(mixT[b], bank[b][:, 0:T], out_a_ready)
                for n, (t0, w) in enumerate(CHUNKS):
                    act.wait_ge(ret_turned, l * 3 + n + 1)
                    copy(qkT[:, :, t0:t0 + w], bank[4 + n][:, 0:4 * w].rearrange("p (c t) -> p c t", c=4), ret_mix)
                layer_norm(l, 0)
                h_feature(2 * l + 1)
                act.wait_ge(ln_ready0, l * 2 + 1)
                act.wait_ge(ln_ready, l * 4 + 2)
                act.dma_start(h_rows[0:META, :], h_tok[0:META, 0, :]).then_inc(h_stored, 16)
                act.dma_start(h_rows[META:T, :].rearrange("(c p) d -> p c d", p=128), h_tok[:, 1:3, :]).then_inc(h_stored, 16)

                act.wait_ge(router_done, l + 1)
                act.wait_ge(moe_clear, l * 2 + 2)
                act.activation(rows3["score"][0:16, 0, :], bank[6][0:16, 0:E], ACT.Sigmoid).then_inc(score_ready, 1)
                act.activation(rows3["score"][:, 1:3, :], bank[6][:, E:3 * E].rearrange("p (c e) -> p c e", c=2),
                               ACT.Sigmoid).then_inc(score_ready, 1)
                for j in range(2):
                    act.wait_ge(shared_done, l * 2 + j + 1)
                    act.activation(sgs[:, j, :], bank[2 * j][:, 0:T], ACT.Sigmoid).then_inc(shared_sig, 1)
                round_(l, 0)
                hold_here(act, count_ready, l + 1)
                most = act.value_load(count_i[0:1, 0:1], min_val=0, max_val=T)
                with act.If(most > CAP):
                    with act.Fori(1, ROUNDS) as r:
                        round_(l, r)
                with act.Else():
                    for s, per in ((sig_ready, 32), (xta_ready, 33), (y_ready, 64)):
                        act.wait_ge(s, l * (ROUNDS * per) + per)
                        act.sem_inc(s, EXTRA * per)
                act.wait_ge(scattered, l * (33 * ROUNDS) + 33 * ROUNDS)
                for b in (0, 2, 4):
                    n = min(512, 8 * T - b * 512)
                    copy(accT[:, b * 512:b * 512 + n], bank[b][:, 0:n], acc_act)
                layer_norm(l, 1)
                h_feature(2 * l + 2)

        @block.vector
        def _(dve):
            steps = [0]

            def step(ins):
                steps[0] += 1
                ins.then_inc(dve_step, 1)

            def after_steps():
                dve.wait_ge(dve_step, steps[0])

            def h_feature(base):
                for j, (n, at) in enumerate(((1, 3), (2, 5))):
                    t0, w = CHUNKS[n]
                    dve.wait_ge(hT_turned, base * 5 + at)
                    dve.tensor_copy(hT[:, 4:8, t0:t0 + w], bank[TURN_BANKS[n][1]][:, 0:4 * w].rearrange("p (k t) -> p k t", k=4))\
                        .then_inc(hT_dve, 1)

            dve.memset(ssq[:], 1.0).then_inc(dve_step, 1)
            dve.memset(ret_mv[:], 1.0).then_inc(dve_step, 1)
            dve.wait_ge(dve_step, 2)
            h_feature(0)

            def layer_norm(l, ph):
                base = l * 6 + ph * 3

                def residual(n):
                    w = CHUNKS[n][1]
                    dve.wait_ge(sub_done, base + n + 1)
                    if ph == 0 and n == 0:
                        parts = [(bank[OUT_BANKS[0][0]][32 * q:32 * q + w, 0:256], q * 256, 256) for q in range(4)]
                    else:
                        banks = OUT_BANKS[n] if ph == 0 else (2 * n, 2 * n + 1)
                        parts = [(bank[b][0:w, :], half * 512, 512) for half, b in enumerate(banks)]
                    for m, (sub, c, cols) in enumerate(parts):
                        step(dve.scalar_tensor_tensor(h_tok[0:w, n, c:c + cols], h_tok[0:w, n, c:c + cols], ALPHA, sub,
                                                      ALU.mult, ALU.add, accum_out=ln_sum[0:w, n, m:m + 1]))
                    after_steps()
                    step(dve.tensor_reduce(ln_neg_mean[0:w, n:n + 1], ln_sum[0:w, n, 0:len(parts)], AX, ALU.add))
                    after_steps()
                    dve.tensor_scalar(ln_neg_mean[0:w, n:n + 1], ln_neg_mean[0:w, n:n + 1], -1.0 / D, None, ALU.mult)\
                        .then_inc(ln_mean_ready, 1)

                def centre(n):
                    w = CHUNKS[n][1]
                    dve.wait_ge(ln_par_in, l * 64 + ph * 32 + 32)
                    dve.wait_ge(ln_mean_ready, base + n + 1)
                    step(dve.scalar_tensor_tensor(ln_scratch[0:w, n, :], h_tok[0:w, n, :], ln_neg_mean[0:w, n:n + 1],
                                                  ln_par[0:w, 0, :], ALU.add, ALU.mult))

                def scale(n):
                    w = CHUNKS[n][1]
                    dve.wait_ge(ln_rstd_ready, base + n + 1)
                    after_steps()
                    dve.scalar_tensor_tensor(h_tok[0:w, n, :], ln_scratch[0:w, n, :], ln_rstd[0:w, n:n + 1],
                                             ln_par[0:w, 1, :], ALU.mult, ALU.add).then_inc(ln_ready, 1)

                residual(0)
                residual(1)
                centre(1)
                residual(2)
                scale(1)
                centre(2)
                scale(2)

            def round_(l, r, extra, shared_hidden=None):
                g = l * ROUNDS + r

                def select(q):
                    dve.wait_ge(slot_row_done, g * 34 + q)
                    at = q * 6
                    dve.tensor_copy(mo["pb"].rearrange("p (c n) -> p c n", c=3),
                                    route_pairs[:, :, bass.ds(at, 6)]).then_inc(pair_ready, 1)
                    dve.wait_ge(pair_ready, g * 34 + q + 1)
                    dve.tensor_tensor(sel.rearrange("p c e s -> p (c e) s"),
                                      k["iota"].unsqueeze(1).to_broadcast([128, 6, CAP]),
                                      pb.rearrange("p c e v -> p (c e) v")[:, :, 2:3].to_broadcast([128, 6, CAP]),
                                      ALU.is_equal).then_inc(sel_ready, 1)

                def slot_rows(q, u):
                    dve.wait_ge(slot_row_done, g * 34 + q + 1)
                    dve.tensor_copy(idg[:, u, :], bank[7][:, 0:2]).then_inc(idg_ready, 1)
                    dve.tensor_scalar(rank_i[:, u:u + 1], bank[7][:, 0:1], FAR, None, ALU.add).then_inc(slot_row_ready, 1)

                def turned(q, u):
                    dve.wait_ge(xtb_done, g * 33 + q + 1)
                    dve.tensor_copy(xgT[:, u, 4:8, :], bank[7][:, :].rearrange("p (k s) -> p k s", k=4)).then_inc(xtb_ready, 1)

                if extra:
                    dve.wait_ge(slot_row_done, g * 34)
                    dve.wait_ge(gather_over, g)
                    dve.tensor_scalar(route[:, :, :, 2], route[:, :, :, 2], -float(CAP), None, ALU.add).then_inc(shifted, 1)
                    dve.wait_ge(shifted, l * EXTRA + r)
                dve.wait_ge(scattered, g * 33)
                dve.memset(selg[:, 1, :], 0.0).then_inc(selg_ready, 1)
                for q in range(2):
                    select(q)
                    slot_rows(q, q)
                if not extra:
                    shared_hidden(1)
                turned(0, 0)
                with dve.Fori(0, PAIRS // 2) as i:
                    for u in range(2):
                        p = i * 2 + u
                        select(p + 2)
                        dve.wait_ge(idg_ready, g * 34 + p + 1)
                        dve.wait_ge(scattered, g * 33 + p)
                        dve.tensor_scalar(selg[:, u, :], k["iota_t"], idg[:, u, 0:1], idg[:, u, 1:2],
                                          ALU.is_equal, ALU.mult).then_inc(selg_ready, 1)
                        dve.wait_ge(selg_ready, g * 33 + p + 2)
                        slot_rows(p + 2, u)
                        dve.wait_ge(sig_ready, g * 32 + p + 1)
                        dve.tensor_tensor(mo["ha"], mo["sg"], bank[5][:, 0:F], ALU.mult).then_inc(ha_ready, 1)
                        dve.wait_ge(gu_done, g * 32 + p + 1)
                        dve.wait_ge(ht_done, g * 32 + p)
                        dve.wait_ge(ha_ready, g * 32 + p + 1)
                        dve.tensor_tensor(mo["h"], mo["ha"], bank[5][:, F:2 * F], ALU.mult).then_inc(h_ready, 1)
                        turned(p + 1, 1 - u)
                        dve.wait_ge(ht_done, g * 32 + p + 1)
                        dve.tensor_copy(mo["h2"], bank[7][:, 0:F]).then_inc(ht_ready, 1)

            with dve.Fori(0, DEPTH) as l:
                steps[0] = 0
                dve.sem_clear(dve_step)

                def proj(b):
                    dve.wait_ge(proj_done, l * 22 + b + 1)
                    dst = qaT[:, b, :] if b < 4 else qiT[:, b - 5, :]
                    dve.tensor_copy(dst, bank[proj_bank(b)][:, 0:T]).then_inc(proj_dve, 1)

                proj(1)
                proj(3)
                for h in (1, 3, 5, 7):
                    dve.wait_ge(lat_done, l * 8 + h + 1)
                    dve.tensor_copy(latT[:, h, :], bank[4 + h % 4][:, 0:T]).then_inc(lat_dve, 1)
                proj(5)
                proj(7)
                dve.wait_ge(ckv_ssq, l * 3 + 3)
                dve.tensor_scalar(ckv_var[:, :], ssq[:, :], 1.0 / LAT, EPS, ALU.mult, ALU.add).then_inc(ckv_var_ready, 1)
                dve.wait_ge(small_mix, l * 64 + 64)
                dve.wait_ge(ckv_rstd_ready, l + 1)
                for n, (t0, w) in enumerate(CHUNKS):
                    dve.scalar_tensor_tensor(ckv[0:w, n, :], bank[4][0:w, n * 128:(n + 1) * 128], ckv_rstd[0:w, n:n + 1],
                                             kvn_w[0:w, :], ALU.mult, ALU.mult).then_inc(ckv_ready, 1)
                dve.wait_ge(proj_done, l * 22 + 10)
                step(dve.tensor_copy(kdT[64:128, :], bank[1][0:64, 0:T]))
                dve.tensor_copy(kwT[0:72, :], bank[1][0:72, 0:T]).then_inc(proj_dve, 1)
                dve.wait_ge(wi_turned, l + 1)
                dve.tensor_scalar(wi[:, 1:3, :], bank[5][:, 72:216].rearrange("p (c n) -> p c n", c=2)[:, :, 64:72],
                                  I_HEADS ** -0.5, None, ALU.mult).then_inc(wi_ready, 1)
                dve.wait_ge(ckvT_done, l + 1)
                dve.tensor_copy(ckvT, bank[6][:, 0:T]).then_inc(ckvT_ready, 1)

                def choose(n, first):
                    K = KEYS[n]
                    wk = work[:, 0:K]
                    for h in range(I_HEADS):
                        m = first + h
                        dve.wait_ge(index_relu, l * 16 + m + 1)
                        dve.wait_ge(wi_ready if h == 0 else index_added, l + 1 if h == 0 else l * 16 + m)
                        dve.scalar_tensor_tensor(wk, rl[:, m % 2, 0:K], wi[:, n, h:h + 1], causal[n] if h == 0 else wk,
                                                 ALU.mult, ALU.add).then_inc(index_added, 1)
                    hold_here(dve, index_added, l * 16 + first + 8)
                    for _ in range(N_SEL // 8):
                        step(dve.max(best8[:, :], wk))
                        after_steps()
                        step(dve.match_replace(wk, best8[:, :], wk, TAKEN))
                        after_steps()
                    step(dve.tensor_scalar(masks[n], wk, -2e38, NEG, ALU.is_gt, ALU.mult))
                    after_steps()
                    step(dve.tensor_tensor(masks[n], masks[n], causal[n], ALU.min))
                    after_steps()

                dve.wait_ge(const_in, 16)
                choose(2, 0)
                choose(1, 8)
                dve.wait_ge(lat_act, l * 4 + 4)
                dve.wait_ge(lat_dve, l * 4 + 4)
                dve.tensor_copy(work[:, 0:128].rearrange("p (h q) -> p h q", h=8), latT[:, :, 0:16]).then_inc(q0_ready, 1)

                for m in range(17 + 4):
                    if m < 17:
                        n = 0 if m == 0 else (2 if m < 9 else 1)
                        hold_here(dve, logits_done, l * 17 + m + 1)
                        if m >= 4:
                            hold_here(dve, prob_turned, l * 17 + m - 3)
                        K = KEYS[n]
                        dve.tensor_tensor_reduce(logit[:, m % 4, 0:K], bank[2 + m % 2][:, 0:K],
                                                 k["causal0"] if n == 0 else masks[n], 1.0, -3e38, ALU.add, ALU.max,
                                                 row_max[:, m:m + 1]).then_inc(logits_masked, 1)
                        dve.wait_ge(logits_masked, l * 17 + m + 1)
                        dve.tensor_scalar(neg_max[:, m:m + 1], row_max[:, m:m + 1], -(A_DIM ** -0.5), None, ALU.mult)\
                            .then_inc(max_ready, 1)
                    if 1 <= m <= 17:
                        dve.wait_ge(exp_done, l * 17 + m)
                        dve.reciprocal(row_inv[:, m - 1:m], row_sum[:, m - 1:m]).then_inc(inv_ready, 1)
                    if m >= 4 and (m - 4) % 4 == 0:
                        grp = (m - 4) // 4
                        dve.wait_ge(olat_done, l * 17 + 4 * grp + 1)
                        if grp == 0:
                            o, i_ = latT[:, :, 0:16], bank[7][:, 0:128].rearrange("p (h q) -> p h q", h=8)
                        else:
                            t0 = CHUNKS[2 if grp <= 2 else 1][0]
                            h0 = 4 * ((grp - 1) % 2)
                            o = latT[:, h0:h0 + 4, t0:t0 + 128]
                            i_ = bank[7 - grp % 2][:, :].rearrange("p (h q) -> p h q", h=4)
                        dve.tensor_copy(o, i_).then_inc(olat_ready, 1)
                for h in range(R_HEADS):
                    b = 2 * (h % 2)
                    dve.wait_ge(ret_scores, l * 8 + 2 * h + 2)
                    if h >= 2:
                        dve.wait_ge(ret_out, l * 4 + h - 1)
                    dec = decayed[:, h % 2, :]
                    dve.tensor_tensor(dec[0:16, 0:T], bank[b][0:16, 0:T], decay[0:16, h, :], ALU.mult).then_inc(ret_decayed, 1)
                    dve.tensor_tensor(dec[:, T:T + 256], bank[b + 1][:, 0:256], decay[:, h, 0:256], ALU.mult)\
                        .then_inc(ret_decayed, 1)
                    dve.tensor_tensor(dec[:, T + 256:T + 384], bank[b + 1][:, 256:384], decay[:, h, 0:128], ALU.mult)\
                        .then_inc(ret_decayed, 1)
                dve.wait_ge(ret_out, l * 4 + 4)
                for n, (t0, w) in enumerate(CHUNKS):
                    for h in range(R_HEADS):
                        step(dve.bn_stats(ret_stats[0:w, 4 * n + h, :], bank[4 + n][0:w, h * 128:(h + 1) * 128]))
                after_steps()
                for n, (t0, w) in enumerate(CHUNKS):
                    for h in range(R_HEADS):
                        step(dve.bn_aggr(ret_mv[0:w, 4 * n + h, :], ret_stats[0:w, 4 * n + h, :]))
                after_steps()
                dve.tensor_scalar(ret_var[:, :], ret_mv[:, :, 1], EPS, None, ALU.add).then_inc(ret_var_ready, 1)
                dve.wait_ge(ret_rstd_ready, l + 1)
                for n, (t0, w) in enumerate(CHUNKS):
                    for h in range(R_HEADS):
                        c = 4 * n + h
                        step(dve.tensor_scalar(o_ret[0:w, n, h * 128:(h + 1) * 128], bank[4 + n][0:w, h * 128:(h + 1) * 128],
                                               ret_mv[0:w, c, 0:1], ret_rstd[0:w, c:c + 1], ALU.subtract, ALU.mult))
                dve.wait_ge(gate_ready, l * 3 + 3)
                after_steps()
                for n, (t0, w) in enumerate(CHUNKS):
                    dve.tensor_tensor(o_ret[0:w, n, :], o_ret[0:w, n, :], gate[0:w, n, :], ALU.mult).then_inc(ret_ready, 1)

                layer_norm(l, 0)
                h_feature(2 * l + 1)

                s3 = rows3
                dve.wait_ge(score_ready, l * 2 + 2)
                dve.wait_ge(small_moe, l * 32 + 32)
                step(dve.tensor_tensor(s3["biased"], s3["score"], rbias[:, :].unsqueeze(1).to_broadcast([128, 3, E]), ALU.add))
                after_steps()
                for n in range(3):
                    for gr in range(GROUPS):
                        step(dve.max(cube["best2"][:, n, gr, :], cube["biased"][:, n, gr, :]))
                after_steps()
                step(dve.tensor_tensor(s3["grp"], cube["best2"][:, :, :, 0], cube["best2"][:, :, :, 1], ALU.add))
                after_steps()
                other = s3["grp"].unsqueeze(2).to_broadcast([128, 3, 8, 8])
                own = s3["grp"].unsqueeze(3).to_broadcast([128, 3, 8, 8])
                step(dve.tensor_tensor(cube["gt"], other, own, ALU.is_gt))
                step(dve.tensor_tensor(cube["eq"], other, own, ALU.is_equal))
                after_steps()
                step(dve.tensor_tensor(mo["eq"].rearrange("p (c n) -> p c n", c=3), mo["eq"].rearrange("p (c n) -> p c n", c=3),
                                       k["tri"].unsqueeze(1).to_broadcast([128, 3, 64]), ALU.mult))
                after_steps()
                step(dve.tensor_tensor(mo["gt"], mo["gt"], mo["eq"], ALU.add))
                after_steps()
                step(dve.tensor_reduce(s3["rank"], cube["gt"], AX, ALU.add))
                after_steps()
                step(dve.tensor_scalar(mo["rank"], mo["rank"], TOP_GROUPS - 0.5, NEG, ALU.is_gt, ALU.mult))
                after_steps()
                step(dve.tensor_tensor(cube["biased"], cube["biased"], s3["rank"].unsqueeze(3).to_broadcast([128, 3, 8, 8]),
                                       ALU.add))
                after_steps()
                for n in range(3):
                    step(dve.max(best8[:, :], s3["biased"][:, n, :]))
                    after_steps()
                    step(dve.match_replace(s3["picked"][:, n, :], best8[:, :], s3["biased"][:, n, :], TAKEN))
                    after_steps()
                dve.tensor_scalar(mo["chosen"], mo["picked"], -2e38, None, ALU.is_le).then_inc(chosen_ready, 1)
                dve.wait_ge(chosen_ready, l + 1)
                step(dve.tensor_tensor(mo["tmp"], mo["score"], mo["chosen"], ALU.mult))
                after_steps()
                step(dve.tensor_reduce(mo["gsum"], s3["tmp"], AX, ALU.add))
                after_steps()
                step(dve.reciprocal(mo["ginv"], mo["gsum"]))
                dve.wait_ge(moe_coded, l + 1)
                after_steps()
                dve.scalar_tensor_tensor(route[:, :, 0:E, 1], s3["tmp"], ROUTE_SCALE,
                                         mo["ginv"].unsqueeze(2).to_broadcast([128, 3, E]), ALU.mult, ALU.mult)\
                    .then_inc(gates_ready, 1)
                def shared_hidden(j):
                    dve.wait_ge(shared_sig, l * 2 + j + 1)
                    step(dve.tensor_tensor(hs[:, j, :], sgs[:, j, :], bank[2 * j][:, 0:T], ALU.mult))
                    after_steps()
                    dve.tensor_tensor(hsT[:, j, :], hs[:, j, :], bank[2 * j + 1][:, 0:T], ALU.mult).then_inc(shared_ready, 1)

                shared_hidden(0)
                dve.wait_ge(rank_done, l + 1)
                b5 = bank[5][:, 0:3 * E].rearrange("p (c e) -> p c e", c=3)
                step(dve.scalar_tensor_tensor(s3["tmp"][0:16, 0, :], b5[0:16, 0, :], 1.0, s3["chosen"][0:16, 0, :],
                                              ALU.add, ALU.mult))
                step(dve.scalar_tensor_tensor(s3["tmp"][:, 1:3, :], b5[:, 1:3, :], 1.0, s3["chosen"][:, 1:3, :],
                                              ALU.add, ALU.mult))
                step(dve.tensor_reduce(mo["cmax"][0:1, :], bank[5][0:1, 3 * E:4 * E], AX, ALU.max))
                after_steps()
                step(dve.tensor_scalar(route[0:16, 0, 0:E, 2], s3["tmp"][0:16, 0, :], -1.0, None, ALU.add))
                dve.tensor_scalar(route[:, 1:3, 0:E, 2], s3["tmp"][:, 1:3, :], -1.0, None, ALU.add).then_inc(rank_ready, 1)
                dve.tensor_copy(count_i[0:1, :], mo["cmax"][0:1, :]).then_inc(count_ready, 1)
                after_steps()
                dve.wait_ge(rank_ready, l + 1)
                dve.wait_ge(gates_ready, l + 1)
                round_(l, 0, False, shared_hidden)
                hold_here(dve, count_ready, l + 1)
                most = dve.value_load(count_i[0:1, 0:1], min_val=0, max_val=T)
                with dve.If(most > CAP):
                    with dve.Fori(1, ROUNDS) as r:
                        round_(l, r, True)
                with dve.Else():
                    dve.sem_inc(shifted, EXTRA)
                    for s, per in ((selg_ready, 33), (pair_ready, 34), (sel_ready, 34), (ha_ready, 32), (h_ready, 32),
                                   (xtb_ready, 33), (ht_ready, 32), (idg_ready, 34), (slot_row_ready, 34)):
                        dve.wait_ge(s, l * (ROUNDS * per) + per)
                        dve.sem_inc(s, EXTRA * per)
                dve.wait_ge(scattered, l * (33 * ROUNDS) + 33 * ROUNDS)
                for b in (1, 3):
                    dve.tensor_copy(accT[:, b * 512:(b + 1) * 512], bank[b][:, :]).then_inc(acc_dve, 1)
                layer_norm(l, 1)
                h_feature(2 * l + 2)

        @block.gpsimd
        def _(pool):
            steps = [0]

            def step(ins):
                steps[0] += 1
                ins.then_inc(pool_step, 1)

            def after_steps():
                pool.wait_ge(pool_step, steps[0])

            rounds_run = pool.alloc_register("rounds_run")
            pool.reg_mov(rounds_run, 0)
            step(pool.memset(half_pow[:, :], -0.5))
            after_steps()
            pool.wait_ge(slot_in[DOUBLE_SLOT[0]], 16)
            pool.dma_start(const[:, 128:N_CONST], a["consts"][:, 128:N_CONST]).then_inc(const_in, 16)

            def layer_norm(l, ph):
                base = l * 6 + ph * 3

                def rstd(n):
                    w = CHUNKS[n][1]
                    hold_here(pool, ln_sq_ready, base + n + 1)
                    step(pool.tensor_scalar(ln_var[0:w, n:n + 1], ln_sq[0:w, n:n + 1], 1.0 / D, EPS, ALU.mult, ALU.add))
                    after_steps()
                    pool.tensor_tensor(ln_rstd[0:w, n:n + 1], ln_var[0:w, n:n + 1], half_pow[0:w, 0:1], ALU.pow)\
                        .then_inc(ln_rstd_ready, 1)

                x = h_tok[0:META, 0, :]
                rstd(0)
                hold_here(pool, ln_rstd_ready, base + 1)
                step(pool.tensor_scalar(x, x, ln_neg_mean[0:META, 0:1], ln_rstd[0:META, 0:1], ALU.add, ALU.mult))
                pool.wait_ge(ln_par_in, l * 64 + ph * 32 + 32)
                after_steps()
                step(pool.tensor_tensor(x, x, ln_par[0:META, 0, :], ALU.mult))
                rstd(1)
                after_steps()
                pool.tensor_tensor(x, x, ln_par[0:META, 1, :], ALU.add).then_inc(ln_ready0, 1)
                rstd(2)

            def load_ln(l, g_, b_):
                for j, src in enumerate((a[g_], a[b_])):
                    pool.dma_start(ln_par[:, j, :], src[bass.ds(l, 1), :].partition_broadcast(128)).then_inc(ln_par_in, 16)

            def round_(l, r, extra):
                g = l * ROUNDS + r

                def gather(q, u, turned):
                    pool.wait_ge(slot_row_ready, g * 34 + q + 1)
                    hold_here(pool, xtb_done, g * 33 + turned)
                    pool.indirect_dma_start(out=xg[:, u, :], out_offset=None, in_=h_rows,
                                            in_offset=bass.IndirectOffsetOnAxis(ap=rank_i[:, u:u + 1], axis=0),
                                            bounds_check=T - 1, oob_is_err=False).then_inc(gathered[u], 16)

                gather(0, 0, 0)
                gather(1, 1, 0)
                if not extra:
                    hold_here(pool, shared_done, l * 2 + 2)
                    pool.memset(y_sb[:, 1, :], 0.0).then_inc(y_clear, 1)
                with pool.Fori(0, PAIRS // 2) as i:
                    for u in range(2):
                        gather(i * 2 + (u + 2), u, i * 2 + (u + 1))
                pool.wait_ge(gathered[1], pool.snap(rounds_run) * (16 * 17) + 16 * 17)
                pool.sem_inc(gather_over, 1)
                pool.reg_add(rounds_run, rounds_run, 1)

            with pool.Fori(0, DEPTH) as l:
                steps[0] = 0
                pool.sem_clear(pool_step)
                pool.dma_start(wuk[:, :, :], a["w_uk"][bass.ds(l, 1)].rearrange("l (j e) d c -> (l e d) j c", e=2))\
                    .then_inc(small_mix, 16)
                pool.dma_start(wuv[:, :, :], a["w_uv"][bass.ds(l, 1)].rearrange("l h c d -> (l c) h d")).then_inc(small_mix, 16)
                pool.dma_start(kvn_w[:, :], a["kv_norm_w"][bass.ds(l, 1), :].partition_broadcast(128)).then_inc(small_mix, 16)
                pool.dma_start(retn_w[:, :], a["ret_norm_w"][bass.ds(l, 1), :].partition_broadcast(128)).then_inc(small_mix, 16)
                pool.dma_start(wr[:, :], a["w_router"][bass.ds(l, 1)].rearrange("l (p k) e -> (l p) (k e)", k=KC))\
                    .then_inc(small_moe, 16)
                pool.dma_start(rbias[:, :], a["router_bias"][bass.ds(l, 1), :].partition_broadcast(128)).then_inc(small_moe, 16)
                load_ln(l, "ln1_g", "ln1_b")
                pool.wait_ge(ckv_var_ready, l + 1)
                pool.tensor_tensor(ckv_rstd[:, :], ckv_var[:, :], half_pow[:, 0:3], ALU.pow).then_inc(ckv_rstd_ready, 1)
                pool.wait_ge(const_in, 16)
                for n, (t0, w) in enumerate(CHUNKS):
                    x = rot[0:w, n, :].rearrange("p (h s f) -> p h s f", h=8, s=2)
                    xa = rot_a[0:w, :].rearrange("p (h s f) -> p h s f", h=8, s=2)
                    xb = rot_b[0:w, :].rearrange("p (h s f) -> p h s f", h=8, s=2)
                    cs = cos3[0:w, n, :].unsqueeze(1).to_broadcast([w, 8, 32])
                    sn = sin3[0:w, n, :].unsqueeze(1).to_broadcast([w, 8, 32])
                    pool.wait_ge(tok_copied, l * 12 + n + 1)
                    for s in range(2):
                        step(pool.tensor_tensor(xa[:, :, s, :], x[:, :, s, :], cs, ALU.mult))
                        step(pool.tensor_tensor(xb[:, :, s, :], x[:, :, 1 - s, :], sn, ALU.mult))
                    after_steps()
                    step(pool.tensor_tensor(x[:, :, 0, :], xa[:, :, 0, :], xb[:, :, 0, :], ALU.subtract))
                    pool.tensor_tensor(x[:, :, 1, :], xa[:, :, 1, :], xb[:, :, 1, :], ALU.add).then_inc(rot_ready, 1)
                    pool.wait_ge(rot_ready, l * 3 + n + 1)
                    after_steps()
                pool.wait_ge(small_mix, l * 64 + 64)
                for n, (t0, w) in enumerate(CHUNKS):
                    pool.wait_ge(gate_sig, l * 3 + n + 1)
                    pool.wait_ge(tok_copied, l * 12 + 7 + n)
                    pool.tensor_tensor(gate[0:w, n, :], gate[0:w, n, :], sg_tmp[0:w, :], ALU.mult).then_inc(gate_mul, 1)
                    pool.wait_ge(gate_mul, l * 3 + n + 1)
                    pool.tensor_tensor(gate[0:w, n, :], gate[0:w, n, :], retn_w[0:w, :], ALU.mult).then_inc(gate_ready, 1)
                pool.wait_ge(ret_var_ready, l + 1)
                pool.tensor_tensor(ret_rstd[:, :], ret_var[:, :], half_pow[:, :], ALU.pow).then_inc(ret_rstd_ready, 1)
                layer_norm(l, 0)
                hold_here(pool, ln_ready0, l * 2 + 1)
                hold_here(pool, ln_ready, l * 4 + 2)
                load_ln(l, "ln2_g", "ln2_b")
                pool.memset(mo["score"], 0.5).then_inc(moe_clear, 1)
                step(pool.memset(mo["route"], -1.0))
                pool.memset(xg[:, :, :], 0.0).then_inc(moe_clear, 1)
                after_steps()
                pool.tensor_copy(route[:, :, :, 0], k["code"].unsqueeze(2).to_broadcast([128, 3, E_PAD])).then_inc(moe_coded, 1)
                pool.wait_ge(moe_clear, l * 2 + 2)
                pool.wait_ge(h_stored, l * 32 + 32)
                round_(l, 0, False)
                hold_here(pool, count_ready, l + 1)
                most = pool.value_load(count_i[0:1, 0:1], min_val=0, max_val=T)
                with pool.If(most > CAP):
                    with pool.Fori(1, ROUNDS) as r:
                        round_(l, r, True)
                with pool.Else():
                    pool.sem_inc(gather_over, EXTRA)
                layer_norm(l, 1)
                pool.wait_ge(ln_ready0, l * 2 + 2)
                pool.wait_ge(ln_ready, l * 4 + 4)


_INS = ["x", "meta_tokens", "w_in", "w_uk", "w_uv", "kv_norm_w", "ret_norm_w", "w_o", "ln1_g", "ln1_b", "w_router",
        "router_bias", "w_gate", "w_up", "w_down", "ws_gate", "ws_up", "ws_down", "ln2_g", "ln2_b"]
_OUTS = [((1, SEQ, D), "float32")]


def kernel(**inputs):
    import numpy as _np
    import concourse.bacc as _bacc
    from concourse import mybir as _mybir
    from concourse.bass_utils import run_bass_kernel_spmd as _run

    nc = _bacc.Bacc("TRN2", target_bir_lowering=False, num_devices=1)
    arrays, aps = {}, {}
    for name in _INS + ["consts"]:
        arr = shape_constants() if name == "consts" else _np.ascontiguousarray(inputs[name])
        arrays[f"in_{name}_dram"] = arr
        aps[name] = nc.dram_tensor(f"in_{name}_dram", arr.shape, _mybir.dt.from_np(arr.dtype), kind="ExternalInput").ap()
    shape, dtype = _OUTS[0]
    out = nc.dram_tensor("out_0_dram", shape, _mybir.dt.from_np(_np.dtype(dtype)), kind="ExternalOutput").ap()
    decoder_kernel(nc, aps, out)
    r = _run(nc, [arrays], core_ids=[0])
    return r.results[0]["out_0_dram"]
```
